# Optimizing a Trainium2 kernel written in Bass

```python
import jax
import jax.numpy as jnp
from jax import lax
import numpy as np

D_MODEL = 1024
BATCH = 1
SEQ = 256
DEPTH = 2

HEAD_DIM = 64
N_BRANCH = 4
ROPE_THETA = 500000.0
PARTIAL_ROT = HEAD_DIM // 4
Q_BLOCK = 128
NORM_EPS = 1e-6

DSA_HEADS = 4
IDX_HEADS = 8
IDX_DIM = 32
IDX_ROT = IDX_DIM // 4
DSA_TOPK_MAX = 256

SB_HEADS = 4

MOBA_HEADS = 4
MOBA_BLOCK = 256
MOBA_TOPK = 3
MOBA_Q_BLOCK = 64

MLA_HEADS = 4
MLA_Q_RANK = 256
MLA_KV_RANK = 128
MLA_NOPE = 64
MLA_ROPE = 32
MLA_V = 64

BRANCH_WIDTH = 4 * HEAD_DIM
D_FF = 4 * D_MODEL

IN_WIDTHS = (
    DSA_HEADS * HEAD_DIM, DSA_HEADS * HEAD_DIM, DSA_HEADS * HEAD_DIM,
    IDX_HEADS * IDX_DIM, IDX_DIM, IDX_HEADS,
    SB_HEADS * HEAD_DIM, SB_HEADS * HEAD_DIM, SB_HEADS * HEAD_DIM,
    MOBA_HEADS * HEAD_DIM, MOBA_HEADS * HEAD_DIM, MOBA_HEADS * HEAD_DIM,
    MLA_Q_RANK, MLA_KV_RANK, MLA_ROPE,
    N_BRANCH * D_MODEL,
)
N_IN = sum(IN_WIDTHS)

kernel_name = 'hybrid_gated_sparse_sb_moba_mla'

def rmsnorm(x, g):
    xf = x.astype(jnp.float32)
    y = xf * lax.rsqrt(jnp.mean(xf * xf, axis=-1, keepdims=True) + NORM_EPS)
    return (y * g.astype(jnp.float32)).astype(x.dtype)

def rope_tables(n_rot, seq):
    inv_freq = 1.0 / (ROPE_THETA ** (jnp.arange(0, n_rot, 2, dtype=jnp.float32) / n_rot))
    ang = jnp.arange(seq, dtype=jnp.float32)[:, None] * inv_freq[None, :]
    return jnp.cos(ang), jnp.sin(ang)

def apply_rope(x, cos, sin):
    n_half = cos.shape[-1]
    n_rot = 2 * n_half
    x1 = x[..., :n_half]
    x2 = x[..., n_half:n_rot]
    c = cos[:, None, :].astype(x.dtype)
    s = sin[:, None, :].astype(x.dtype)
    return jnp.concatenate([x1 * c - x2 * s, x2 * c + x1 * s, x[..., n_rot:]], axis=-1)

def to_heads(a, n):
    return a.reshape(a.shape[0], a.shape[1], n, a.shape[2] // n)

def split_columns(z):
    offsets = []
    acc = 0
    for w in IN_WIDTHS[:-1]:
        acc += w
        offsets.append(acc)
    return jnp.split(z, offsets, axis=-1)

def sweep_query_blocks(block_fn, n_blocks):
    out = lax.map(block_fn, jnp.arange(n_blocks))
    nb, b, qb, h, d = out.shape
    return out.transpose(1, 0, 2, 3, 4).reshape(b, nb * qb, h, d)

def dsa_attention(q, k, v, qi, ki, wi):
    S = q.shape[1]
    top = min(DSA_TOPK_MAX, S // 4)
    scale = HEAD_DIM ** -0.5
    key_pos = jnp.arange(S)
    gather = jax.vmap(lambda kk, ii: kk[ii])

    def block(i):
        start = i * Q_BLOCK
        t = start + jnp.arange(Q_BLOCK)
        qb = lax.dynamic_slice_in_dim(q, start, Q_BLOCK, axis=1)
        qib = lax.dynamic_slice_in_dim(qi, start, Q_BLOCK, axis=1)
        wib = lax.dynamic_slice_in_dim(wi, start, Q_BLOCK, axis=1).astype(jnp.float32)
        rel = jax.nn.relu(jnp.einsum('bqhd,bsd->bqhs', qib, ki).astype(jnp.float32) * (IDX_DIM ** -0.5))
        score = jnp.einsum('bqhs,bqh->bqs', rel, wib * (IDX_HEADS ** -0.5))
        causal = key_pos[None, :] <= t[:, None]
        score = jnp.where(causal[None], score, -jnp.inf)
        _, sel = lax.top_k(score, top)
        valid = sel <= t[None, :, None]
        kg = gather(k, sel)
        vg = gather(v, sel)
        logits = jnp.einsum('bqhd,bqkhd->bhqk', qb, kg).astype(jnp.float32) * scale
        logits = jnp.where(valid[:, None], logits, -jnp.inf)
        p = jax.nn.softmax(logits, axis=-1).astype(v.dtype)
        return jnp.einsum('bhqk,bqkhd->bqhd', p, vg)

    return sweep_query_blocks(block, S // Q_BLOCK)

def stick_breaking_attention(q, k, v):
    S = q.shape[1]
    scale = HEAD_DIM ** -0.5
    key_pos = jnp.arange(S)

    def block(i):
        start = i * Q_BLOCK
        t = start + jnp.arange(Q_BLOCK)
        qb = lax.dynamic_slice_in_dim(q, start, Q_BLOCK, axis=1)
        z = jnp.einsum('bqhd,bshd->bhqs', qb, k).astype(jnp.float32) * scale
        past = key_pos[None, :] < t[:, None]
        log_fail = jnp.where(past, jax.nn.log_sigmoid(-z), 0.0)
        later = lax.cumsum(log_fail, axis=3, reverse=True) - log_fail
        a = jnp.where(past, jnp.exp(jax.nn.log_sigmoid(z) + later), 0.0)
        return jnp.einsum('bhqs,bshd->bqhd', a.astype(v.dtype), v)

    return sweep_query_blocks(block, S // Q_BLOCK)

def moba_attention(q, k, v):
    B, S, H, dh = q.shape
    nb = -(-S // MOBA_BLOCK)
    s_pad = nb * MOBA_BLOCK
    n_sel = min(MOBA_TOPK, nb)
    scale = dh ** -0.5
    pad = ((0, 0), (0, s_pad - S), (0, 0), (0, 0))
    kp = jnp.pad(k, pad)
    vp = jnp.pad(v, pad)
    kblk = kp.reshape(B, nb, MOBA_BLOCK, H, dh).transpose(0, 3, 1, 2, 4)
    vblk = vp.reshape(B, nb, MOBA_BLOCK, H, dh).transpose(0, 3, 1, 2, 4)
    kmean = jnp.mean(kblk.astype(jnp.float32), axis=3).astype(k.dtype)
    gather = jax.vmap(jax.vmap(lambda kk, ii: kk[ii]))
    blk_ids = jnp.arange(nb)

    def block(i):
        start = i * MOBA_Q_BLOCK
        t = start + jnp.arange(MOBA_Q_BLOCK)
        own = start // MOBA_BLOCK
        qb = lax.dynamic_slice_in_dim(q, start, MOBA_Q_BLOCK, axis=1)
        gate = jnp.einsum('bqhd,bhnd->bhqn', qb, kmean).astype(jnp.float32)
        gate = jnp.where(blk_ids < own, gate, -jnp.inf)
        _, sel = lax.top_k(gate, n_sel)
        valid = sel < own
        kg = gather(kblk, sel)
        vg = gather(vblk, sel)
        l_sel = jnp.einsum('bqhd,bhqnld->bhqnl', qb, kg).astype(jnp.float32) * scale
        l_sel = jnp.where(valid[..., None], l_sel, -jnp.inf).reshape(B, H, MOBA_Q_BLOCK, n_sel * MOBA_BLOCK)
        k_own = lax.dynamic_slice_in_dim(kp, own * MOBA_BLOCK, MOBA_BLOCK, axis=1)
        v_own = lax.dynamic_slice_in_dim(vp, own * MOBA_BLOCK, MOBA_BLOCK, axis=1)
        l_own = jnp.einsum('bqhd,bshd->bhqs', qb, k_own).astype(jnp.float32) * scale
        own_pos = own * MOBA_BLOCK + jnp.arange(MOBA_BLOCK)
        l_own = jnp.where(own_pos[None, :] <= t[:, None], l_own, -jnp.inf)
        p = jax.nn.softmax(jnp.concatenate([l_sel, l_own], axis=-1), axis=-1).astype(v.dtype)
        p_sel = p[..., :n_sel * MOBA_BLOCK].reshape(B, H, MOBA_Q_BLOCK, n_sel, MOBA_BLOCK)
        p_own = p[..., n_sel * MOBA_BLOCK:]
        return (jnp.einsum('bhqnl,bhqnld->bqhd', p_sel, vg)
                + jnp.einsum('bhqs,bshd->bqhd', p_own, v_own))

    return sweep_query_blocks(block, S // MOBA_Q_BLOCK)

def mla_attention(q_nope, q_rope, k_nope, k_rope, v):
    S = q_nope.shape[1]
    scale = (MLA_NOPE + MLA_ROPE) ** -0.5
    key_pos = jnp.arange(S)

    def block(i):
        start = i * Q_BLOCK
        t = start + jnp.arange(Q_BLOCK)
        qn = lax.dynamic_slice_in_dim(q_nope, start, Q_BLOCK, axis=1)
        qr = lax.dynamic_slice_in_dim(q_rope, start, Q_BLOCK, axis=1)
        logits = (jnp.einsum('bqhd,bshd->bhqs', qn, k_nope)
                  + jnp.einsum('bqhr,bsr->bhqs', qr, k_rope)).astype(jnp.float32) * scale
        logits = jnp.where(key_pos[None, :] <= t[:, None], logits, -jnp.inf)
        p = jax.nn.softmax(logits, axis=-1).astype(v.dtype)
        return jnp.einsum('bhqs,bshd->bqhd', p, v)

    return sweep_query_blocks(block, S // Q_BLOCK)

def setup_inputs(seed: int = 0) -> dict:
    key = jax.random.key(seed)
    ks = jax.random.split(key, 14)
    f32 = jnp.float32

    def nrm(k, shape, scale):
        return jax.random.normal(k, shape, f32) * scale

    return {
        'x': nrm(ks[0], (BATCH, SEQ, D_MODEL), 1.0),
        'norm_mix': 1.0 + nrm(ks[1], (DEPTH, D_MODEL), 0.05),
        'w_in': nrm(ks[2], (DEPTH, D_MODEL, N_IN), D_MODEL ** -0.5),
        'b_gate': nrm(ks[3], (DEPTH, N_BRANCH, D_MODEL), 0.1),
        'mla_q_norm': 1.0 + nrm(ks[4], (DEPTH, MLA_Q_RANK), 0.05),
        'mla_kv_norm': 1.0 + nrm(ks[5], (DEPTH, MLA_KV_RANK), 0.05),
        'w_uq': nrm(ks[6], (DEPTH, MLA_Q_RANK, MLA_HEADS * (MLA_NOPE + MLA_ROPE)), MLA_Q_RANK ** -0.5),
        'w_ukv': nrm(ks[7], (DEPTH, MLA_KV_RANK, MLA_HEADS * (MLA_NOPE + MLA_V)), MLA_KV_RANK ** -0.5),
        'w_branch': nrm(ks[8], (DEPTH, N_BRANCH, BRANCH_WIDTH, D_MODEL), BRANCH_WIDTH ** -0.5),
        'w_out': nrm(ks[9], (DEPTH, D_MODEL, D_MODEL), D_MODEL ** -0.5),
        'norm_mlp': 1.0 + nrm(ks[10], (DEPTH, D_MODEL), 0.05),
        'w_up': nrm(ks[11], (DEPTH, D_MODEL, D_FF), D_MODEL ** -0.5),
        'w_down': nrm(ks[12], (DEPTH, D_FF, D_MODEL), D_FF ** -0.5),
        'norm_final': 1.0 + nrm(ks[13], (D_MODEL,), 0.05),
    }

def reference(x, norm_mix, w_in, b_gate, mla_q_norm, mla_kv_norm, w_uq, w_ukv,
              w_branch, w_out, norm_mlp, w_up, w_down, norm_final):
    B, S, _ = x.shape
    cos_p, sin_p = rope_tables(PARTIAL_ROT, S)
    cos_i, sin_i = rope_tables(IDX_ROT, S)
    cos_m, sin_m = rope_tables(MLA_ROPE, S)

    for l in range(DEPTH):
        h = rmsnorm(x, norm_mix[l])
        z = h @ w_in[l]
        (dq, dk, dv, iq, ik, iw, sq, sk, sv, mq, mk, mv,
         cq, ckv, kr, gate_logits) = split_columns(z)

        o_a = dsa_attention(
            apply_rope(to_heads(dq, DSA_HEADS), cos_p, sin_p),
            apply_rope(to_heads(dk, DSA_HEADS), cos_p, sin_p),
            to_heads(dv, DSA_HEADS),
            apply_rope(to_heads(iq, IDX_HEADS), cos_i, sin_i),
            apply_rope(ik[:, :, None, :], cos_i, sin_i)[:, :, 0],
            iw)

        o_b = stick_breaking_attention(to_heads(sq, SB_HEADS), to_heads(sk, SB_HEADS),
                                       to_heads(sv, SB_HEADS))

        o_c = moba_attention(apply_rope(to_heads(mq, MOBA_HEADS), cos_p, sin_p),
                             apply_rope(to_heads(mk, MOBA_HEADS), cos_p, sin_p),
                             to_heads(mv, MOBA_HEADS))

        qu = to_heads(rmsnorm(cq, mla_q_norm[l]) @ w_uq[l], MLA_HEADS)
        kvu = to_heads(rmsnorm(ckv, mla_kv_norm[l]) @ w_ukv[l], MLA_HEADS)
        o_d = mla_attention(qu[..., :MLA_NOPE],
                            apply_rope(qu[..., MLA_NOPE:], cos_m, sin_m),
                            kvu[..., :MLA_NOPE],
                            apply_rope(kr[:, :, None, :], cos_m, sin_m)[:, :, 0],
                            kvu[..., MLA_NOPE:])

        branches = jnp.stack([o_a.reshape(B, S, -1), o_b.reshape(B, S, -1),
                              o_c.reshape(B, S, -1), o_d.reshape(B, S, -1)], axis=2)
        gates = jax.nn.sigmoid(gate_logits.reshape(B, S, N_BRANCH, D_MODEL) + b_gate[l])
        proj = jnp.einsum('bsnc,ncd->bsnd', branches, w_branch[l])
        merged = jnp.sum(gates * proj, axis=2)
        x = x + merged @ w_out[l]

        h2 = rmsnorm(x, norm_mlp[l])
        x = x + jnp.square(jax.nn.relu(h2 @ w_up[l])) @ w_down[l]

    return rmsnorm(x, norm_final)


_drawn_inputs = setup_inputs


def setup_inputs(seed=0):
    import zlib

    import numpy as np

    out = dict(_drawn_inputs(seed))
    spreads = {}
    factors = {'mla_q_norm': 8.0, 'mla_kv_norm': 4.388}
    for name, (base, spread) in spreads.items():
        noise = np.random.default_rng([zlib.crc32(name.encode()), seed]).standard_normal(out[name].shape)
        drawn = base * np.exp(spread * noise) if base else spread * noise
        out[name] = jnp.asarray(drawn.astype(out[name].dtype))
    for name, factor in factors.items():
        out[name] = (out[name] * factor).astype(out[name].dtype)
    return out
```

```python
from contextlib import ExitStack

import concourse.bass as bass
from concourse import mybir

DEPTH, SEQ, D_MODEL, D_FF = 2, 256, 1024, 4096
P = 128
TT = SEQ // P
KT = D_MODEL // P
HEAD_DIM, N_BRANCH, HEADS = 64, 4, 4
IDX_HEADS, IDX_DIM, IDX_TOP = 8, 32, SEQ // 4
MLA_Q, MLA_KV, MLA_NOPE, MLA_ROPE = 256, 128, 64, 32
MLA_QK = MLA_NOPE + MLA_ROPE
NORM_EPS, ROPE_THETA = 1e-6, 500000.0
BW = HEADS * HEAD_DIM
GATE0 = 3016

GROUPS = [(1024, 296), (2856, 160), (2344, 512), (1320, 512), (512, 512), (1832, 512), (0, 512)]
IK, IW, SQ, CKV, KR, CQ, SK, IQ, MQ, MK, DQ, DK, ZW = 0, 32, 40, 296, 424, 456, 712, 968, 1224, 1480, 1736, 1992, 2248

CHUNKS = [("group", g, half) for g in range(6) for half in range(2)] + [("uq",), ("ukv",)]
CHUNKS += [("group", 6, 0), ("group", 6, 1)]
CHUNKS += [("gate", j) for j in range(16)]
PROJ_ORDER = [1, 2, 3, 0]
CHUNKS += [("branch", n) for n in range(N_BRANCH)]
CHUNKS += [("out", half, kh) for half in range(2) for kh in range(2)]
CHUNKS += [("up", 0)] + [x for j in range(15) for x in (("up", j + 1), ("down", j))] + [("down", 15)]
NCH = len(CHUNKS)
CW = 2048
C_GATE, C_BRANCH, C_OUT, C_MLP = 16, 32, 36, 40
RING = 3
FF_STEPS = D_FF // 256


def chunk_width(c):
    kind = CHUNKS[c]
    if kind[0] == "group":
        return 4 * GROUPS[kind[1]][1]
    return {"uq": 2 * HEADS * MLA_QK, "ukv": HEADS * 2 * MLA_NOPE}.get(kind[0], CW)


SMALL_AT = [0]
for _c in range(C_GATE):
    SMALL_AT.append(SMALL_AT[-1] + P * chunk_width(_c))

CONSTS = dict(ident=128, negsuf=128, negones=128, causal=128, past=128, rope=TT * 56, num=2)
CONST_AT, CONST_W = {}, 0
for _n, _w in CONSTS.items():
    CONST_AT[_n] = CONST_W
    CONST_W += _w
NEG, TAKEN = -1.0e30, -3.0e38
GAIN_MIX, GAIN_MLP, GAIN_Q, GAIN_KV, GAIN_W = 0, 1024, 2048, 2304, 2432


def psum_plan():
    jobs, fills = {}, [0] * 8

    def add(job, bank):
        jobs[job] = (bank, fills[bank])
        fills[bank] += 1

    stream = [("hT", q) for q in range(4)]
    for g in range(6):
        stream += [("group", g, 0), ("group", g, 1)]
    stream += [("uq", 0), ("uq", 1), ("ukv", 0), ("ukv", 1), ("group", 6, 0), ("group", 6, 1)]
    stream += [("gate", j) for j in range(16)]
    stream += [("proj", n, q) for n in range(N_BRANCH) for q in range(4)]
    stream += [("out", half, tt) for half in range(2) for tt in range(TT)]
    stream += [("h2T", q) for q in range(4)]
    for n, job in enumerate(stream):
        add(job, n % 4)
    for j in range(FF_STEPS):
        add(("up", j), j % 3)
    for tt in range(TT):
        for half in range(2):
            add(("down", tt, half), 4 + 2 * tt + half)
    for n, name in enumerate(["sq", "ik", "ckv", "sk", "cq", "iq", "mq", "mk", "mlaq0", "mlaq1", "mlak0", "mlak1"]):
        add(("T", name), 4 + n % 4)
    for qt in (1, 0):
        for r in range(4):
            add(("idx", qt, r), 4 + r)
    add(("T", "dq"), 6)
    add(("T", "dk"), 7)
    for s in range(16):
        add(("S", s), 4 + s % 2)
        if s >= 4:
            add(("PT", s), 6)
        if s % 2:
            add(("O", s // 2), 7)
    return jobs, fills


JOBS, FILLS = psum_plan()


def used_plan():
    plan, count = [], 0
    for kind in CHUNKS:
        fills = {"group": ("group", *kind[1:2], 1), "uq": ("uq", 1), "ukv": ("ukv", 1), "gate": kind,
                 "branch": ("proj", kind[-1], 3), "out": ("out", *kind[1:2], 1), "up": kind}.get(kind[0])
        if fills is None or (kind[0] in ("group", "out") and kind[2] == 0):
            count += kind != ("down", FF_STEPS - 1)
            plan.append([None, count, None])
        else:
            b, turn = JOBS[fills]
            plan.append([b, turn + 1, FILLS[b]])
    return [(b, n, count if b is None else per) for b, n, per in plan], count


USED_BY, CHUNKS_USED = used_plan()

SQUARES, NORMED = 12, 12
NORMS, ROPES, POOL_LINKS, ACT_LINKS = 8, 6, 6 + 2 * 4 + 4, 8


def build(nc, x, w_small, w_big, gains, gate_bias, consts, out):
    F32, F32R, BF16 = mybir.dt.float32, mybir.dt.float32r, mybir.dt.bfloat16
    ALU, ACT, AX = mybir.AluOpType, mybir.ActivationFunctionType, mybir.AxisListType
    ctx = ExitStack()
    with ctx:
        def sb(name, shape, dt=F32, where=ctx):
            return where.enter_context(nc.sbuf_tensor(name, shape, dt))

        def sem(name):
            return ctx.enter_context(nc.semaphore(name))

        x_sb = sb("x_sb", [P, TT, D_MODEL])
        gain = sb("gain", [P, GAIN_W])
        bias = sb("bias", [P, 32])
        cst = sb("cst", [P, CONST_W])
        ident_bf = sb("ident_bf", [P, P], BF16)
        causal_bf = sb("causal_bf", [P, P], BF16)
        past_bf = sb("past_bf", [P, P], BF16)
        stage = sb("stage", [P, RING, CW])
        w_hi = sb("w_hi", [P, RING, CW], F32R)
        w_lo = sb("w_lo", [P, RING, CW], F32R)
        aT_hi = sb("aT_hi", [P, KT, SEQ], F32R)
        aT_lo = sb("aT_lo", [P, KT, SEQ], F32R)
        sumsq = sb("sumsq", [P, NORMS, 2])
        mean = sb("mean", [P, 2, NORMS])
        rstd = sb("rstd", [P, NORMS])
        values = sb("values", [P, TT, 3, BW])
        v_mla = sb("v_mla", [P, TT, BW])
        mla_qT = sb("mla_qT", [P, HEADS, SEQ])
        mla_kT = sb("mla_kT", [P, HEADS, SEQ])
        probs = sb("probs", [P, 2, 384])
        probsT = sb("probsT", [P, 2, 384])
        rowmax = sb("rowmax", [P, 2, 2])
        negmax = sb("negmax", [P, 2, 2])
        rowsum = sb("rowsum", [P, 2, 2])
        rowinv = sb("rowinv", [P, 2, 2])
        oT_hi = sb("oT_hi", [P, 8, SEQ], F32R)
        oT_lo = sb("oT_lo", [P, 8, SEQ], F32R)
        rel = sb("rel", [P, 2, 512])
        score = [sb(f"score{n}", [P, 384]) for n in range(2)]
        top8 = sb("top8", [P, 2, 8])
        idx_w = sb("idx_w", [P, TT, IDX_HEADS])
        dsa_mask = sb("dsa_mask", [P, 384], BF16)
        rope_tmp = sb("rope_tmp", [P, 4, 128])
        qk_region = sb("qk_region", [P, 15 * 256])

        def piece(n, blocks=2):
            return qk_region[:, 512 * n:512 * n + 256 * blocks].rearrange("p (b t) -> p b t", t=SEQ)

        sqT, skT, mqT, mkT, dqT, dkT, iqT = (piece(n) for n in range(7))
        ikT = qk_region[:, 14 * 256:15 * 256]
        merged = qk_region[:, 0:2048].rearrange("p (f t) -> p f t", t=SEQ)
        product = qk_region[:, 2048:3584].rearrange("p (a n) -> p a n", a=3)
        junk = [qk_region[:, D_MODEL * t:D_MODEL * t + D_MODEL] for t in range(TT)]
        small_junk = [qk_region[:, 2048 + 256 * n:2304 + 256 * n] for n in range(4)]
        with ExitStack() as first:
            zq = sb("zq", [P, TT, ZW], where=first)
            q_cat = sb("q_cat", [P, TT, HEADS * MLA_QK], where=first)
            k_cat = sb("k_cat", [P, TT, HEADS * MLA_QK], where=first)
            c_norm = sb("c_norm", [P, TT, 384], where=first)
            ik_rep = sb("ik_rep", [P, TT, 4, IDX_DIM], where=first)
            cT_hi = sb("cT_hi", [P, 3, SEQ], F32R, where=first)
            cT_lo = sb("cT_lo", [P, 3, SEQ], F32R, where=first)
        with ExitStack() as second:
            gates = sb("gates", [P, 16, 512], where=second)
        with ExitStack() as third:
            xn = sb("xn", [P, TT, D_MODEL], where=third)
            act_sq = sb("act_sq", [P, 3, 512], where=third)
            uT_hi = sb("uT_hi", [P, 3, 512], F32R, where=third)
            uT_lo = sb("uT_lo", [P, 3, 512], F32R, where=third)

        bank = [ctx.enter_context(nc.psum_tensor(f"bank{n}", [P, 512], F32)) for n in range(8)]

        def const(name, a=0, b=None):
            at = CONST_AT[name]
            return cst[:, at + a:at + (CONSTS[name] if b is None else b)]

        ident, negsuf, negones, causal = (const(n) for n in ("ident", "negsuf", "negones", "causal"))
        rope_tab = const("rope").rearrange("p (t n) -> p t n", t=TT)

        loaded = [sem(f"loaded{n}") for n in range(RING)]
        x_loaded, consts_loaded = sem("x_loaded"), sem("consts_loaded")
        mix_loaded = sem("mix_loaded")
        gains_loaded = sem("gains_loaded")
        hi_ready = sem("hi_ready")
        lo_ready = sem("lo_ready")
        chunk_used = sem("chunk_used")
        filled = [sem(f"filled{n}") for n in range(8)]
        drained = [sem(f"drained{n}") for n in range(8)]
        squares_ready = sem("squares_ready")
        rstd_ready = sem("rstd_ready")
        normed_ready = sem("normed_ready")
        a_hi_ready = sem("a_hi_ready")
        merged_lo_ready = sem("merged_lo_ready")
        c_hi_ready = sem("c_hi_ready")
        roped = sem("roped")
        pool_link, act_link, dve_link = sem("pool_link"), sem("act_link"), sem("dve_link")
        rel_used = sem("rel_used")
        mask_ready = sem("mask_ready")
        ln_ready = sem("ln_ready")
        negmax_ready = sem("negmax_ready")
        probs_ready = sem("probs_ready")
        cum_done = sem("cum_done")
        first_of_pair = sem("first_of_pair")
        o_hi_ready = sem("o_hi_ready")
        gates_ready = sem("gates_ready")
        pool_sums = sem("pool_sums")
        merged_ready = sem("merged_ready")
        relu_ready = sem("relu_ready")
        u_hi_ready, u_lo_ready = sem("u_hi_ready"), sem("u_lo_ready")
        const_ready = sem("const_ready")
        stored = sem("stored")

        ONE = 1

        def wait_filled(e, l, job, more=0):
            b, turn = JOBS[job]
            e.wait_ge(filled[b], l * FILLS[b] + ONE + turn + 1 + more)

        def wait_drained(e, l, job, more=0):
            b, turn = JOBS[job]
            e.wait_ge(drained[b], l * FILLS[b] + ONE + turn + 1 + more)

        def wait_empty(e, l, job, more=0):
            b, turn = JOBS[job]
            e.wait_ge(drained[b], l * FILLS[b] + ONE + turn + more)

        def wait_read(e, l, jobs, empty=None):
            need = {}
            for job in jobs:
                b, turn = JOBS[job]
                need[b] = max(need.get(b, 0), turn + 1)
            if empty is not None:
                b, turn = JOBS[empty]
                need[b] = max(need.get(b, 0), turn)
            for b, turn in need.items():
                e.wait_ge(drained[b], l * FILLS[b] + ONE + turn)

        def wait_chunk_used(e, l, c, more=0):
            if CHUNKS[c][0] == "down" and CHUNKS[c][1] == FF_STEPS - 1:
                wait_filled(e, l, ("down", 1, 1))
                return
            signal, count, per_layer = USED_BY[c % NCH]
            e.wait_ge(chunk_used if signal is None else filled[signal],
                      l * per_layer + ONE + count - (per_layer if c < 0 else 0) + more)

        def wait_head_done(e, l, s):
            if s % 2:
                wait_filled(e, l, ("O", s // 2))
            else:
                e.wait_ge(first_of_pair, l * 8 + s // 2 + 1)

        def bank_of(job):
            return bank[JOBS[job][0]]

        def filled_of(job):
            return filled[JOBS[job][0]]

        def drained_of(job):
            return drained[JOBS[job][0]]

        def four(b):
            return b[:, :].rearrange("p (a t) -> p a t", t=P)

        def a_tiles(aT, q):
            return aT[:, 4 * (q % 2):4 * (q % 2) + 4, P * (q // 2):P * (q // 2) + P]

        def two(ap):
            return ap.rearrange("p (a t) -> p a t", t=SEQ)

        SB_KIND, MOBA_KIND, MLA_KIND, DSA_KIND = range(4)

        def head_scale(s):
            return float(MLA_QK) ** -0.5 if s // 4 == MLA_KIND else 1.0

        def group_pieces(g, tt, b):
            if g == 0:
                rep = b[:, 8:IDX_DIM].unsqueeze(1).to_broadcast([P, 4, IDX_DIM - 8])
                return [(ik_rep[:, tt, :, 8:IDX_DIM], rep), (zq[:, tt, IK:IK + 296], b[:, 0:296])]
            if g == 1:
                return [(zq[:, tt, CKV:CKV + 160], b[:, 0:160])]
            if g in (5, 6):
                at = MQ if g == 5 else DQ
                return [(zq[:, tt, at:at + 512], b[:, :])]
            v, at, first = {2: (1, CQ, True), 3: (0, SK, False), 4: (2, IQ, True)}[g]
            a, c = (0, 256) if first else (256, 0)
            return [(values[:, tt, v, :], b[:, a:a + 256]), (zq[:, tt, at:at + 256], b[:, c:c + 256])]

        def evac_uq(e, l, tt):
            job = ("uq", tt)
            wait_filled(e, l, job)
            if tt == 0:
                e.activation(q_cat[:, tt, :], bank_of(job)[:, 0:384], ACT.Copy).then_inc(drained_of(job), 1)
            else:
                e.tensor_copy(q_cat[:, tt, :], bank_of(job)[:, 0:384]).then_inc(drained_of(job), 1)

        def evac_ukv(e, l, tt):
            job = ("ukv", tt)
            wait_filled(e, l, job)
            kv = bank_of(job)[:, :].rearrange("p (h d) -> p h d", h=HEADS)
            k_to = k_cat[:, tt, :].rearrange("p (h d) -> p h d", h=HEADS)[:, :, 0:MLA_NOPE]
            v_to = v_mla[:, tt, :].rearrange("p (h d) -> p h d", h=HEADS)
            if tt == 0:
                e.activation(k_to, kv[:, :, 0:MLA_NOPE], ACT.Copy)
                e.activation(v_to, kv[:, :, MLA_NOPE:128], ACT.Copy).then_inc(drained_of(job), 1)
            else:
                e.tensor_copy(k_to, kv[:, :, 0:MLA_NOPE])
                e.tensor_copy(v_to, kv[:, :, MLA_NOPE:128]).then_inc(drained_of(job), 1)

        block = ctx.enter_context(nc.Block())

        @block.sync
        def _(sp):
            for tt in range(TT):
                sp.dma_start(x_sb[:, tt, :], x[0, P * tt:P * tt + P, :]).then_inc(x_loaded, 16)

            def load(l, c):
                sp.wait_ge(lo_ready, l * NCH + c + 1)
                if c < C_GATE:
                    n = chunk_width(c)
                    src = w_small[l, SMALL_AT[c]:SMALL_AT[c + 1]].rearrange("(p n) -> p n", n=n)
                    sp.dma_start(stage[:, c % RING, 0:n], src).then_inc(loaded[c % RING], 16)
                else:
                    sp.dma_start(stage[:, c % RING, :], w_big[l, c - C_GATE, :, :]).then_inc(loaded[c % RING], 16)

            def load_mix_gain(l):
                sp.dma_start(gain[:, 0:GAIN_MLP], gains[l, 0:GAIN_MLP].partition_broadcast(P)).then_inc(mix_loaded, 16)

            def load_gains(l):
                sp.dma_start(gain[:, GAIN_MLP:], gains[l, GAIN_MLP:].partition_broadcast(P)).then_inc(gains_loaded, 16)
                sp.dma_start(bias[:, :], gate_bias[l, :, :]).then_inc(gains_loaded, 16)

            load_mix_gain(0)
            sp.dma_start(cst[:, :], consts).then_inc(consts_loaded, 16)
            with sp.Fori(0, DEPTH) as l:
                for c in range(4):
                    load(l, c)
                sp.wait_ge(normed_ready, l * NORMED + 2)
                load_gains(l)
                for c in range(4, C_MLP + 3):
                    load(l, c)
                with sp.Fori(0, 4) as i:
                    for c in range(C_MLP + 3, C_MLP + 9):
                        sp.wait_ge(lo_ready, l * NCH + i * 6 + c + 1)
                        sp.dma_start(stage[:, c % RING, :], w_big[l, i * 6 + (c - C_GATE), :, :])\
                          .then_inc(loaded[c % RING], 16)
                for c in range(C_MLP + 27, NCH):
                    load(l, c)
                sp.wait_ge(normed_ready, l * NORMED + 4)
                load_mix_gain(l + 1)
            sp.wait_ge(normed_ready, DEPTH * NORMED + 2 * TT)
            sp.dma_start(out.rearrange("b (t p) d -> p (b t) d", p=P), xn[:, :, :]).then_inc(stored, 16)
            sp.wait_ge(stored, 16)

        @block.gpsimd
        def _(pool):
            pool.wait_ge(consts_loaded, 16)

            def norm_factor(l, n):
                halves = n in (0, 1, 6, 7)
                squares = {0: 1, 1: 3, 2: 5, 3: 6, 4: 7, 5: 8, 6: 9, 7: 11}[n]
                pool.wait_ge(squares_ready, l * SQUARES + squares)
                links = NORM_LINK[n]
                pool.tensor_tensor(mean[:, 0, n:n + 1], sumsq[:, n, 0:1], const("num", 0, 1), ALU.add)\
                    .then_inc(pool_link, 1)
                pool.wait_ge(pool_link, l * POOL_LINKS + links + 1)
                if halves:
                    pool.wait_ge(squares_ready, l * SQUARES + squares + 1)
                    pool.tensor_tensor(mean[:, 1, n:n + 1], mean[:, 0, n:n + 1], sumsq[:, n, 1:2], ALU.add)\
                        .then_inc(pool_link, 1)
                    pool.wait_ge(pool_link, l * POOL_LINKS + links + 2)
                pool.tensor_tensor(rstd[:, n:n + 1], mean[:, 1 if halves else 0, n:n + 1], const("num", 1, 2), ALU.pow)\
                    .then_inc(rstd_ready, 1)

            NORM_LINK = {0: 0, 1: 2, 2: 6, 3: 7, 4: 8, 5: 9, 6: 14, 7: 16}
            ROPE_LINK = {"ik": 4, "kr": 5, "iq": 10, "m": 11, "mlaq": 12, "d": 13}

            def rope(l, name, src, heads, half, tab, dst=None, copies=1):
                x1, x2 = src[:, :, :, 0:half], src[:, :, :, half:2 * half]
                cos = rope_tab[:, :, tab:tab + half].unsqueeze(2).to_broadcast([P, TT, heads, half])
                sin = rope_tab[:, :, tab + half:tab + 2 * half].unsqueeze(2).to_broadcast([P, TT, heads, half])
                n = TT * heads * half
                tmp = [rope_tmp[:, k, 0:n].rearrange("p (t h d) -> p t h d", t=TT, h=heads) for k in range(4)]
                pool.wait_ge(roped, l * ROPES + ONE + list(ROPE_LINK).index(name))
                pool.tensor_tensor(tmp[0], x1, cos, ALU.mult)
                pool.tensor_tensor(tmp[1], x2, sin, ALU.mult)
                pool.tensor_tensor(tmp[2], x2, cos, ALU.mult)
                pool.tensor_tensor(tmp[3], x1, sin, ALU.mult).then_inc(pool_link, 1)
                pool.wait_ge(pool_link, l * POOL_LINKS + ROPE_LINK[name] + 1)
                if copies > 1:
                    tmp = [t.to_broadcast([P, TT, copies, half]) for t in tmp]
                d = src if dst is None else dst
                pool.tensor_tensor(d[:, :, :, 0:half], tmp[0], tmp[1], ALU.subtract)
                pool.tensor_tensor(d[:, :, :, half:2 * half], tmp[2], tmp[3], ALU.add).then_inc(roped, 1)

            def group_there(l, g):
                for tt in range(TT):
                    wait_drained(pool, l, (*g, tt))

            def heads_of(a, n, dim):
                return zq[:, :, a:a + n * dim].rearrange("p t (h d) -> p t h d", d=dim)

            with pool.Fori(0, DEPTH) as l:
                for tt in range(TT):
                    norm_factor(l, tt)
                group_there(l, ("group", 0))
                rope(l, "ik", heads_of(IK, 1, IDX_DIM), 1, 4, 16, dst=ik_rep, copies=4)
                group_there(l, ("group", 1))
                rope(l, "kr", heads_of(KR, 1, MLA_ROPE), 1, 16, 24,
                     dst=k_cat[:, :, :].rearrange("p t (h d) -> p t h d", h=HEADS)[:, :, :, MLA_NOPE:MLA_QK], copies=4)
                for n in (2, 3):
                    norm_factor(l, n)
                for n in (4, 5):
                    norm_factor(l, n)
                group_there(l, ("group", 4))
                rope(l, "iq", heads_of(IQ, IDX_HEADS, IDX_DIM), IDX_HEADS, 4, 16)
                group_there(l, ("group", 5))
                rope(l, "m", heads_of(MQ, 8, HEAD_DIM), 8, 8, 0)
                group_there(l, ("uq",))
                rope(l, "mlaq", q_cat[:, :, :].rearrange("p t (h d) -> p t h d", h=HEADS)[:, :, :, MLA_NOPE:MLA_QK],
                     HEADS, 16, 24)
                group_there(l, ("group", 6))
                rope(l, "d", heads_of(DQ, 8, HEAD_DIM), 8, 8, 0)
                for k in range(8):
                    wait_drained(pool, l, ("proj", 1 + k // 4, k % 4))
                    if k >= 4:
                        pool.wait_ge(pool_sums, l * 8 + k - 3)
                    m = qk_region[:, 512 * (k % 4):512 * (k % 4) + 512]
                    pool.tensor_tensor(m, m, product[:, k % 3, :], ALU.add).then_inc(pool_sums, 1)
                for n in (6, 7):
                    norm_factor(l, n)
            for tt in range(TT):
                norm_factor(DEPTH, tt)

        @block.scalar
        def _(act):

            def split_hi(l, c, i=None):
                n, more = (chunk_width(c), 0) if i is None else (CW, i * (1 if CHUNKS[c - RING][0] == "up" else 3))
                act.wait_ge(loaded[c % RING], (l * (NCH // RING) + c // RING + 1 + (0 if i is None else i * 2)) * 16)
                wait_chunk_used(act, l, c - RING, more)
                act.activation(w_hi[:, c % RING, 0:n], stage[:, c % RING, 0:n], ACT.Copy).then_inc(hi_ready, 1)

            def x_squares(l, n, after):
                for half in range(2):
                    wait_drained(act, l, after(n % 2, half))
                    cols = slice(512 * half, 512 * half + 512)
                    act.activation(junk[n % 2][:, cols], x_sb[:, n % 2, cols], ACT.Square, scale=D_MODEL ** -0.5,
                                   accum_out=sumsq[:, n, half:half + 1]).then_inc(squares_ready, 1)

            def c_squares(l, n, tt, at, width):
                wait_drained(act, l, ("group", 1 if at == CKV else 2, tt))
                act.activation(small_junk[n - 2][:, 0:width], zq[:, tt, at:at + width], ACT.Square,
                               scale=float(width) ** -0.5, accum_out=sumsq[:, n, 0:1]).then_inc(squares_ready, 1)

            def a_hi(l, name, q):
                job = (name, q)
                wait_filled(act, l, job)
                act.activation(a_tiles(aT_hi, q), four(bank_of(job)), ACT.Copy).then_inc(a_hi_ready, 1)

            def evac_group(l, g):
                job = ("group", g, 0)
                wait_filled(act, l, job)
                b = bank_of(job)
                for k, (dst, src) in enumerate(group_pieces(g, 0, b)):
                    last = act.activation(dst, src, ACT.Copy)
                last.then_inc(drained_of(job), 1)

            def evac_t(l, name, dst, rows=P, scale=1.0):
                job = ("T", name)
                wait_filled(act, l, job)
                act.activation(dst, two(bank_of(job)[0:rows, :]), ACT.Copy, scale=scale).then_inc(drained_of(job), 1)

            def c_hi(l, name, a, n):
                job = ("T", name)
                wait_filled(act, l, job)
                act.activation(cT_hi[:, a:a + n, :], two(bank_of(job)[:, 0:256 * n]), ACT.Copy).then_inc(c_hi_ready, 1)

            def head_finish(l, s):
                if s >= 2:
                    wait_head_done(act, l, s - 2)
                if s // 4 == SB_KIND:
                    act.wait_ge(cum_done, l * 4 + s + 1)
                    act.activation(probsT[:, s % 2, :], bank_of(("S", s))[:, 0:384], ACT.Exp)\
                       .then_inc(drained_of(("S", s)), 1)
                else:
                    wait_filled(act, l, ("PT", s))
                    act.activation(probsT[:, s % 2, :], bank_of(("PT", s))[:, 0:384], ACT.Copy)\
                       .then_inc(drained_of(("PT", s)), 1)

            def head_start(l, s):
                S, pr = bank_of(("S", s)), probs[:, s % 2, :]
                if s // 4 == SB_KIND:
                    wait_filled(act, l, ("S", s))
                    act.activation(pr, S[:, 0:384], ACT.Abs).then_inc(act_link, 1)
                    act.wait_ge(act_link, l * ACT_LINKS + 2 * s + 1)
                    act.activation(pr, pr, ACT.Exp, scale=-1.0).then_inc(act_link, 1)
                    act.wait_ge(act_link, l * ACT_LINKS + 2 * s + 2)
                    act.activation(pr, pr, ACT.Ln, bias=1.0).then_inc(ln_ready, 1)
                else:
                    act.wait_ge(negmax_ready, l * 12 + s - 3)
                    for qt, (a, b) in enumerate(((0, 128), (128, 384))):
                        last = act.activation(pr[:, a:b], S[:, a:b], ACT.Exp, bias=negmax[:, s % 2, qt:qt + 1],
                                              scale=head_scale(s), accum_out=rowsum[:, s % 2, qt:qt + 1])
                    last.then_inc(drained_of(("S", s)), 1)

            def gate_logits(l, j):
                job = ("gate", j)
                wait_filled(act, l, job)
                for f in range(2):
                    last = act.activation(gates[:, j, 256 * f:256 * f + 256], bank_of(job)[:, 256 * f:256 * f + 256],
                                          ACT.Identity, bias=bias[:, 2 * j + f:2 * j + f + 1])
                last.then_inc(drained_of(job), 1)

            def sigmoid(l, n):
                b = PROJ_ORDER[n]
                wait_drained(act, l, ("gate", 15))
                act.activation(gates[:, 4 * b:4 * b + 4, :], gates[:, 4 * b:4 * b + 4, :], ACT.Sigmoid)\
                   .then_inc(gates_ready, 1)

            def o_hi(l, p):
                wait_head_done(act, l, 2 * p + 1)
                act.activation(oT_hi[:, p, :], bank_of(("O", p))[:, 0:256], ACT.Copy).then_inc(o_hi_ready, 1)

            with act.Fori(0, DEPTH) as l:
                split_hi(l, 0)
                for tt in range(TT):
                    x_squares(l, tt, lambda tt, half: ("down", tt, half))
                for q in range(4):
                    a_hi(l, "hT", q)
                split_hi(l, 1)
                for c in range(C_GATE):
                    if c == 2:
                        evac_group(l, 0)
                    if c == 4:
                        evac_group(l, 1)
                        for tt in range(TT):
                            c_squares(l, 2 + tt, tt, CKV, MLA_KV)
                    if c == 5:
                        evac_t(l, "sq", sqT, scale=0.125)
                    if c == 6:
                        evac_group(l, 2)
                        for tt in range(TT):
                            c_squares(l, 4 + tt, tt, CQ, MLA_Q)
                    if c == 7:
                        c_hi(l, "ckv", 2, 1)
                    if c == 8:
                        evac_group(l, 3)
                    if c == 9:
                        c_hi(l, "cq", 0, 2)
                    if c == 10:
                        evac_group(l, 4)
                    if c == 12:
                        evac_group(l, 5)
                    if c == 13:
                        evac_uq(act, l, 0)
                        evac_t(l, "iq", iqT)
                    if c == 14:
                        evac_ukv(act, l, 0)
                    if c == 15:
                        evac_t(l, "mq", mqT, scale=0.125)
                    split_hi(l, c + 2)
                evac_group(l, 6)
                for h in range(2):
                    evac_t(l, f"mlaq{h}", mla_qT[0:MLA_QK, 2 * h:2 * h + 2, :], rows=MLA_QK)
                for qt in (1, 0):
                    for r in range(4):
                        job = ("idx", qt, r)
                        n = 4 * (1 - qt) + r
                        wait_filled(act, l, job)
                        if n >= 2:
                            act.wait_ge(rel_used, l * 8 + n - 1)
                        w = 256 * (1 + qt)
                        act.activation(rel[:, n % 2, 0:w], bank_of(job)[:, 0:w], ACT.Relu,
                                       scale=float(IDX_DIM) ** -0.5).then_inc(drained_of(job), 1)
                evac_t(l, "dq", dqT, scale=0.125)
                act.preload_act_table_set("natural_log_exp_and_others")
                for s in range(16):
                    if s >= 1:
                        head_finish(l, s - 1)
                    head_start(l, s)
                    if s >= 1:
                        gate_logits(l, s - 1)
                    if s >= 3 and s % 2 == 1:
                        o_hi(l, (s - 2) // 2)
                    split_hi(l, C_GATE + s + 2)
                head_finish(l, 15)
                gate_logits(l, 15)
                sigmoid(l, 0)
                split_hi(l, C_BRANCH + 2)
                sigmoid(l, 1)
                o_hi(l, 7)
                split_hi(l, C_BRANCH + 3)
                sigmoid(l, 2)
                split_hi(l, C_BRANCH + 4)
                sigmoid(l, 3)
                split_hi(l, C_BRANCH + 5)
                for q in range(4):
                    act.wait_ge(merged_ready, l * 4 + q + 1)
                    act.activation(aT_hi[:, 2 * q:2 * q + 2, :], merged[:, 2 * q:2 * q + 2, :], ACT.Copy)\
                       .then_inc(a_hi_ready, 1)
                for k in range(4):
                    split_hi(l, C_OUT + k + 2)
                for tt in range(TT):
                    x_squares(l, 6 + tt, lambda tt, half: ("out", half, tt))
                for q in range(4):
                    a_hi(l, "h2T", q)
                split_hi(l, C_MLP + 2)

                def mlp(k, i=None):
                    more = 0 if i is None else i
                    job = ("up", k)
                    wait_filled(act, l, job, more)
                    act.activation(act_sq[:, k % 3, :], bank_of(job)[:, :], ACT.Relu).then_inc(relu_ready, 1)
                    if C_MLP + 3 + 2 * k < NCH:
                        split_hi(l, C_MLP + 3 + 2 * k, i)
                    wait_drained(act, l, job, more)
                    act.activation(uT_hi[:, k % 3, :], act_sq[:, k % 3, :], ACT.Copy).then_inc(u_hi_ready, 1)
                    if C_MLP + 4 + 2 * k < NCH:
                        split_hi(l, C_MLP + 4 + 2 * k, i)

                mlp(0)
                with act.Fori(0, 4) as i:
                    for k in (1, 2, 3):
                        mlp(k, i)
                for k in (13, 14, 15):
                    mlp(k)
            for tt in range(TT):
                x_squares(DEPTH, tt, lambda tt, half: ("down", tt, half))


        @block.vector
        def _(dve):
            links = [0]

            def link(ins):
                links[0] += 1
                ins.then_inc(dve_link, 1)
                dve.wait_ge(dve_link, links[0])

            for count in (*filled, *drained, chunk_used, roped):
                dve.sem_inc(count, ONE)
            for b in range(4, 8):
                dve.memset(bank[b][:, :], 0.0).then_inc(filled[b], 1)
            dve.wait_ge(consts_loaded, 16)
            dve.tensor_copy(ident_bf[:, :], ident).then_inc(lo_ready, RING)
            dve.tensor_copy(causal_bf[:, :], causal)
            dve.tensor_copy(past_bf[:, :], const("past")).then_inc(const_ready, 1)
            dve.wait_ge(x_loaded, 32)

            def split_lo(l, c, i=None):
                n, more = (chunk_width(c), 0) if i is None else (CW, i * 6)
                dve.wait_ge(hi_ready, l * NCH + c + 1 + more)
                dve.tensor_tensor(w_lo[:, c % RING, 0:n], stage[:, c % RING, 0:n],
                                  w_hi[:, c % RING, 0:n].bitcast(F32), ALU.subtract).then_inc(lo_ready, 1)

            def residual(l, tt, half, job):
                wait_filled(dve, l, job)
                xs = x_sb[:, tt, 512 * half:512 * half + 512]
                dve.tensor_tensor(xs, bank_of(job)[:, :], xs, ALU.add).then_inc(drained_of(job), 1)

            def x_norm(l, n, gain_at):
                dve.wait_ge(rstd_ready, l * NORMS + n + 1)
                for half in range(2):
                    cols = slice(512 * half, 512 * half + 512)
                    dve.scalar_tensor_tensor(xn[:, n % 2, cols], x_sb[:, n % 2, cols], rstd[:, n:n + 1],
                                             gain[:, gain_at + 512 * half:gain_at + 512 * half + 512],
                                             ALU.mult, ALU.mult).then_inc(normed_ready, 1)

            def add_and_norm(l, name, jobs, first, gain_at, n):
                for tt, half in ((0, 0), (0, 1), (1, 0)):
                    residual(l, tt, half, jobs(tt, half))
                x_norm(l, first, gain_at)
                residual(l, 1, 1, jobs(1, 1))
                for tt in range(TT):
                    if tt:
                        x_norm(l, first + tt, gain_at)
                    if name is not None:
                        for q in (2 * tt, 2 * tt + 1):
                            a_lo(l, name, q, n)

            def c_norm_of(l, n, tt, at, to, width, gain_at):
                dve.wait_ge(rstd_ready, l * NORMS + n + 1)
                dve.scalar_tensor_tensor(c_norm[:, tt, to:to + width], zq[:, tt, at:at + width], rstd[:, n:n + 1],
                                         gain[:, gain_at:gain_at + width], ALU.mult, ALU.mult)\
                   .then_inc(normed_ready, 1)

            def a_lo(l, name, q, n):
                job = (name, q)
                dve.wait_ge(a_hi_ready, l * 12 + n + q + 1)
                dve.tensor_tensor(a_tiles(aT_lo, q), four(bank_of(job)), a_tiles(aT_hi, q).bitcast(F32),
                                  ALU.subtract).then_inc(drained_of(job), 1)

            def evac_group(l, g):
                job = ("group", g, 1)
                wait_filled(dve, l, job)
                for dst, src in group_pieces(g, 1, bank_of(job)):
                    last = dve.tensor_copy(dst, src)
                last.then_inc(drained_of(job), 1)

            def evac_t(l, name, dst, rows=P, w=512):
                job = ("T", name)
                wait_filled(dve, l, job)
                src = bank_of(job)[0:rows, 0:w]
                dve.tensor_copy(dst, two(src) if w == 512 else src).then_inc(drained_of(job), 1)

            def c_lo(l, name, a, n):
                job = ("T", name)
                dve.wait_ge(c_hi_ready, l * 2 + (1 if name == "ckv" else 2))
                dve.tensor_tensor(cT_lo[:, a:a + n, :], two(bank_of(job)[:, 0:256 * n]),
                                  cT_hi[:, a:a + n, :].bitcast(F32), ALU.subtract).then_inc(drained_of(job), 1)

            SPAN = {0: (0, 128), 1: (128, 384)}

            def index_scores(l):
                n = 0
                for qt in (1, 0):
                    a, b = SPAN[qt]
                    w, acc = b - a, score[0][:, a:b]
                    for r in range(4):
                        wait_drained(dve, l, ("idx", qt, r))
                        w0, w1 = (idx_w[:, qt, h:h + 1] for h in (r, r + 4))
                        if r == 0:
                            link(dve.tensor_scalar(acc, rel[:, n % 2, 0:w], w0, None, ALU.mult))
                        else:
                            link(dve.scalar_tensor_tensor(acc, rel[:, n % 2, 0:w], w0, acc, ALU.mult, ALU.add))
                        dve.scalar_tensor_tensor(acc, rel[:, n % 2, w:2 * w], w1, acc, ALU.mult, ALU.add)\
                           .then_inc(rel_used, 1)
                        n += 1
                        dve.wait_ge(rel_used, l * 8 + n)
                    link(dve.tensor_tensor(score[0][:, b - 128:b], score[0][:, b - 128:b], causal, ALU.add))

            def top_round(n):
                for qt in (1, 0):
                    link(dve.max(top8[:, qt, :], score[n % 2][:, slice(*SPAN[qt])]))
                    link(dve.match_replace(score[1 - n % 2][:, slice(*SPAN[qt])], top8[:, qt, :],
                                           score[n % 2][:, slice(*SPAN[qt])], TAKEN))

            def index_mask():
                link(dve.tensor_scalar(score[1][:, :], score[0][:, :], TAKEN, NEG, ALU.not_equal, ALU.mult))
                dve.tensor_copy(dsa_mask[:, 128:256], score[1][:, 128:256])
                dve.tensor_tensor(dsa_mask[:, 0:128], score[1][:, 0:128], causal, ALU.add)
                dve.tensor_tensor(dsa_mask[:, 256:384], score[1][:, 256:384], causal, ALU.add).then_inc(mask_ready, 1)

            def head_max(l, s):
                S = bank_of(("S", s))
                wait_filled(dve, l, ("S", s))
                dve.reduce_max(rowmax[:, s % 2, 0:1], S[:, 0:128], AX.X)
                link(dve.reduce_max(rowmax[:, s % 2, 1:2], S[:, 128:384], AX.X))
                dve.tensor_scalar(negmax[:, s % 2, :], rowmax[:, s % 2, :], -head_scale(s), None, ALU.mult)\
                   .then_inc(negmax_ready, 1)

            def head_norm(l, s):
                wait_drained(dve, l, ("S", s))
                link(dve.reciprocal(rowinv[:, s % 2, :], rowsum[:, s % 2, :]))
                for qt in range(2):
                    a, b = SPAN[qt]
                    last = dve.tensor_scalar(probs[:, s % 2, a:b], probs[:, s % 2, a:b],
                                             rowinv[:, s % 2, qt:qt + 1], None, ALU.mult)
                last.then_inc(probs_ready, 1)

            def softplus(l, s):
                dve.wait_ge(ln_ready, l * 4 + s + 1)
                dve.scalar_tensor_tensor(probs[:, s % 2, :], bank_of(("S", s))[:, 0:384], 0.0, probs[:, s % 2, :],
                                         ALU.max, ALU.add).then_inc(probs_ready, 1)

            def o_lo(l, p):
                dve.wait_ge(o_hi_ready, l * 8 + p + 1)
                dve.tensor_tensor(oT_lo[:, p, :], bank_of(("O", p))[:, 0:256], oT_hi[:, p, :].bitcast(F32),
                                  ALU.subtract).then_inc(drained_of(("O", p)), 1)

            def merge(l, n, q):
                job = ("proj", n, q)
                g = gates[:, 4 * PROJ_ORDER[n] + q, :]
                m = qk_region[:, 512 * q:512 * q + 512]
                wait_filled(dve, l, job)
                if n == 0:
                    dve.tensor_tensor(m, bank_of(job)[:, :], g, ALU.mult).then_inc(drained_of(job), 1)
                    return
                k = 4 * (n - 1) + q
                if k >= 3:
                    dve.wait_ge(*((pool_sums, l * 8 + k - 2) if k <= 10 else (merged_ready, l * 4 + 1)))
                dve.tensor_tensor(product[:, k % 3, :], bank_of(job)[:, :], g, ALU.mult).then_inc(drained_of(job), 1)
                if n == N_BRANCH - 1:
                    wait_drained(dve, l, job)
                    dve.wait_ge(pool_sums, l * 8 + 4 + q + 1)
                    dve.tensor_tensor(m, m, product[:, k % 3, :], ALU.add).then_inc(merged_ready, 1)

            def merged_lo(l, q):
                dve.wait_ge(a_hi_ready, l * 12 + 4 + q + 1)
                dve.tensor_tensor(aT_lo[:, 2 * q:2 * q + 2, :], merged[:, 2 * q:2 * q + 2, :],
                                  aT_hi[:, 2 * q:2 * q + 2, :].bitcast(F32), ALU.subtract)\
                   .then_inc(merged_lo_ready, 1)

            with dve.Fori(0, DEPTH) as l:
                dve.sem_clear(dve_link)
                split_lo(l, 0)
                dve.wait_ge(mix_loaded, l * 16 + 16)
                add_and_norm(l, "hT", lambda tt, half: ("down", tt, half), 0, GAIN_MIX, 0)
                split_lo(l, 1)
                dve.wait_ge(gains_loaded, l * 32 + 32)
                for c in range(C_GATE):
                    if c == 2:
                        evac_group(l, 0)
                    if c == 3:
                        for tt in range(TT):
                            wait_drained(dve, l, ("group", 0, tt))
                        dve.tensor_scalar(idx_w[:, :, :], zq[:, :, IW:IW + 8], float(IDX_HEADS) ** -0.5, None, ALU.mult)
                    if c == 4:
                        evac_group(l, 1)
                    if c == 5:
                        evac_t(l, "ik", ikT, w=256)
                        for tt in range(TT):
                            c_norm_of(l, 2 + tt, tt, CKV, MLA_Q, MLA_KV, GAIN_KV)
                    if c == 6:
                        evac_group(l, 2)
                    if c == 7:
                        for tt in range(TT):
                            c_norm_of(l, 4 + tt, tt, CQ, 0, MLA_Q, GAIN_Q)
                        c_lo(l, "ckv", 2, 1)
                    if c == 8:
                        evac_group(l, 3)
                    if c == 9:
                        evac_t(l, "sk", skT)
                        c_lo(l, "cq", 0, 2)
                    if c == 10:
                        evac_group(l, 4)
                    if c == 12:
                        evac_group(l, 5)
                    if c == 13:
                        evac_uq(dve, l, 1)
                    if c == 14:
                        evac_ukv(dve, l, 1)
                    if c == 15:
                        evac_t(l, "mk", mkT)
                    split_lo(l, c + 2)
                evac_group(l, 6)
                for h in range(2):
                    evac_t(l, f"mlak{h}", mla_kT[0:MLA_QK, 2 * h:2 * h + 2, :], rows=MLA_QK)
                index_scores(l)
                evac_t(l, "dk", dkT)
                for s in range(16):
                    if s >= 4:
                        head_max(l, s)
                    if 1 <= s <= 8:
                        top_round(s - 1)
                    if s == 9:
                        index_mask()
                    if s < 4:
                        softplus(l, s)
                    else:
                        head_norm(l, s)
                    if s >= 3 and s % 2 == 1:
                        o_lo(l, (s - 2) // 2)
                    split_lo(l, C_GATE + s + 2)
                for n in range(N_BRANCH):
                    if n == 1:
                        o_lo(l, 7)
                    dve.wait_ge(gates_ready, l * 4 + n + 1)
                    merge(l, n, 0)
                    if n < N_BRANCH - 1:
                        split_lo(l, C_BRANCH + n + 2)
                    for q in range(1, 4):
                        merge(l, n, q)
                        if n == N_BRANCH - 1 and q >= 2:
                            merged_lo(l, q - 2)
                for q in (2, 3):
                    merged_lo(l, q)
                split_lo(l, C_BRANCH + 5)
                for k in range(4):
                    split_lo(l, C_OUT + k + 2)
                add_and_norm(l, "h2T", lambda tt, half: ("out", half, tt), 6, GAIN_MLP, 8)
                split_lo(l, C_MLP + 2)

                def mlp(k, i=None):
                    more = 0 if i is None else i
                    job = ("up", k)
                    dve.wait_ge(relu_ready, l * FF_STEPS + k + 1 + 3 * more)
                    dve.scalar_tensor_tensor(act_sq[:, k % 3, :], bank_of(job)[:, :], 0.0, act_sq[:, k % 3, :],
                                             ALU.max, ALU.mult).then_inc(drained_of(job), 1)
                    if C_MLP + 3 + 2 * k < NCH:
                        split_lo(l, C_MLP + 3 + 2 * k, i)
                    dve.wait_ge(u_hi_ready, l * FF_STEPS + k + 1 + 3 * more)
                    dve.tensor_tensor(uT_lo[:, k % 3, :], act_sq[:, k % 3, :], uT_hi[:, k % 3, :].bitcast(F32),
                                      ALU.subtract).then_inc(u_lo_ready, 1)
                    if C_MLP + 4 + 2 * k < NCH:
                        split_lo(l, C_MLP + 4 + 2 * k, i)

                mlp(0)
                with dve.Fori(0, 4) as i:
                    for k in (1, 2, 3):
                        mlp(k, i)
                for k in (13, 14, 15):
                    mlp(k)
            dve.wait_ge(mix_loaded, DEPTH * 16 + 16)
            add_and_norm(DEPTH, None, lambda tt, half: ("down", tt, half), 0, GAIN_MIX, 0)

        @block.tensor
        def _(pe):
            pe.wait_ge(const_ready, 1)

            def products(dst, a_hi, a_lo, b_hi, b_lo, start, stop):
                pe.matmul(dst, a_hi, b_lo, start=start, stop=False)
                pe.matmul(dst, a_hi, b_hi, start=False, stop=False)
                return pe.matmul(dst, a_lo, b_hi, start=False, stop=stop)

            def wait_chunk(l, c, i=None):
                pe.wait_ge(lo_ready, l * NCH + RING + c + 1 + (0 if i is None else i * 6))

            def weights(c, width):
                n = chunk_width(c)
                return [w[:, c % RING, 0:n].rearrange("p (k f) -> p k f", f=width) for w in (w_hi, w_lo)]

            def x_transposes(l, name, n):
                for q in range(4):
                    tt, job = q // 2, (name, q)
                    pe.wait_ge(normed_ready, l * NORMED + n + q + 1)
                    wait_empty(pe, l, job)
                    for k in range(4):
                        at = P * (4 * (q % 2) + k)
                        last = pe.transpose(bank_of(job)[:, P * k:P * k + P], xn[:, tt, at:at + P], ident)
                    last.then_inc(filled_of(job), 1)

            def group_half(l, c):
                _, g, half = CHUNKS[c]
                width = GROUPS[g][1]
                hi, lo = weights(c, width)
                wait_chunk(l, c)
                for tt in range(TT):
                    job = ("group", g, tt)
                    if half == 0:
                        wait_empty(pe, l, job)
                    for kk in range(4):
                        k = 4 * half + kk
                        if g == 0 and kk == 0:
                            wait_drained(pe, l, ("hT", 2 * tt + half))
                        t = slice(P * tt, P * tt + P)
                        last = products(bank_of(job)[:, 0:width], aT_hi[:, k, t], aT_lo[:, k, t],
                                        hi[:, kk, :], lo[:, kk, :], k == 0, k == KT - 1)
                    if half == 1:
                        last.then_inc(filled_of(job), 1)
                if half == 0:
                    last.then_inc(chunk_used, 1)

            def latent(l, c, name, width, first, n):
                hi, lo = weights(c, width)
                wait_chunk(l, c)
                for tt in range(TT):
                    job = (name, tt)
                    wait_read(pe, l, [("T", "cq" if name == "uq" else "ckv")], empty=job)
                    t = slice(P * tt, P * tt + P)
                    for k in range(n):
                        last = products(bank_of(job)[:, 0:width], cT_hi[:, first + k, t], cT_lo[:, first + k, t],
                                        hi[:, k, :], lo[:, k, :], k == 0, k == n - 1)
                    last.then_inc(filled_of(job), 1)

            def transposes(l, name, blocks):
                job = ("T", name)
                wait_empty(pe, l, job)
                for n, block_of in enumerate(blocks):
                    for tt in range(TT):
                        src = block_of(tt)
                        last = pe.transpose(bank_of(job)[0:src.shape[1], 256 * n + P * tt:256 * n + P * tt + P], src, ident)
                last.then_inc(filled_of(job), 1)

            def z_blocks(at, n=2):
                return [lambda tt, a=at + P * k: zq[:, tt, a:a + P] for k in range(n)]

            def wait_group(l, g):
                for tt in range(TT):
                    wait_drained(pe, l, ("group", g, tt))

            def index_products(l):
                pe.wait_ge(roped, l * ROPES + ONE + 3)
                for qt in (1, 0):
                    w = P * (qt + 1)
                    for r in range(4):
                        job = ("idx", qt, r)
                        wait_read(pe, l, [("T", "iq"), ("T", "ik")] if (qt, r) == (1, 0) else [], empty=job)
                        rows = slice(32 * r, 32 * r + 32)
                        for b in range(2):
                            last = pe.matmul(bank_of(job)[:, w * b:w * b + w], iqT[rows, b, P * qt:P * qt + P],
                                             ikT[rows, 0:w], start=True, stop=True)
                        last.then_inc(filled_of(job), 1)

            def head_operands(s):
                kind, h = s // 4, s % 4
                if kind == MLA_KIND:
                    return mla_qT[0:MLA_QK, h, :], mla_kT[0:MLA_QK, h, :]
                q, k = {SB_KIND: (sqT, skT), MOBA_KIND: (mqT, mkT), DSA_KIND: (dqT, dkT)}[kind]
                rows = slice(64 * (h % 2), 64 * (h % 2) + 64)
                return q[rows, h // 2, :], k[rows, h // 2, :]

            def head_logits(l, s):
                job = ("S", s)
                S, (q, k) = bank_of(job), head_operands(s)
                kind = s // 4
                names = ()
                if s % 4 == 0:
                    names = {SB_KIND: ("sq", "sk"), MOBA_KIND: ("mq", "mk"),
                             MLA_KIND: ("mlaq0", "mlaq1", "mlak0", "mlak1"), DSA_KIND: ("dq", "dk")}[kind]
                    if kind == DSA_KIND:
                        pe.wait_ge(mask_ready, l + 1)
                wait_read(pe, l, [("T", name) for name in names], empty=job)
                if kind == SB_KIND:
                    pe.matmul(S[:, 0:256], k[:, 0:128], q[:, 0:256], start=True, stop=False, skip_group_check=True)
                    pe.matmul(S[:, 256:384], k[:, 128:256], q[:, 128:256], start=False, stop=False, skip_group_check=True)
                    pe.matmul(S[:, 0:128], ident_bf[:, :], past_bf[:, :], start=False, stop=False, skip_group_check=True)
                    last = pe.matmul(S[:, 256:384], ident_bf[:, :], past_bf[:, :], start=False, stop=False,
                                     skip_group_check=True)
                else:
                    pe.matmul(S[:, 0:128], q[:, 0:128], k[:, 0:128], start=True, stop=False)
                    pe.matmul(S[:, 0:128], ident_bf[:, :],
                              dsa_mask[:, 0:128] if kind == DSA_KIND else causal_bf[:, :], start=False, stop=True)
                    pe.matmul(S[:, 128:384], q[:, 128:256], k[:, 0:256], start=True, stop=False)
                    if kind == DSA_KIND:
                        last = pe.matmul(S[:, 128:384], ident_bf[:, :], dsa_mask[:, 128:384], start=False, stop=True)
                    else:
                        last = pe.matmul(S[:, 256:384], ident_bf[:, :], causal_bf[:, :], start=False, stop=True)
                last.then_inc(filled_of(job), 1)

            def head_turn(l, s):
                pe.wait_ge(probs_ready, l * 16 + s + 1)
                pr = probs[:, s % 2, :]
                if s // 4 == SB_KIND:
                    S = bank_of(("S", s))
                    pe.matmul(S[:, 0:256], negsuf, pr[:, 0:256], start=False, stop=False, skip_group_check=True)
                    pe.matmul(S[:, 128:256], negones, pr[:, 256:384], start=False, stop=False, skip_group_check=True)
                    pe.matmul(S[:, 256:384], negsuf, pr[:, 256:384], start=False, stop=True, skip_group_check=True)\
                      .then_inc(cum_done, 1)
                    return
                job = ("PT", s)
                wait_empty(pe, l, job)
                for n in range(3):
                    last = pe.transpose(bank_of(job)[:, P * n:P * n + P], pr[:, P * n:P * n + P], ident)
                last.then_inc(filled_of(job), 1)

            def head_values(l, s):
                kind, h = s // 4, s % 4
                job = ("O", s // 2)
                wait_read(pe, l, [("S", s) if kind == SB_KIND else ("PT", s)], empty=job if s % 2 == 0 else None)
                v = v_mla if kind == MLA_KIND else values[:, :, {SB_KIND: 0, MOBA_KIND: 1, DSA_KIND: 2}[kind], :]
                cols = slice(64 * h, 64 * h + 64)
                o = bank_of(job)[64 * (s % 2):64 * (s % 2) + 64, :]
                pT = probsT[:, s % 2, :]
                pe.matmul(o[:, 0:256], v[:, 0, cols], pT[:, 0:256], start=True, stop=False)
                pe.matmul(o[:, 128:256], v[:, 1, cols], pT[:, 256:384], start=False, stop=True)\
                  .then_inc(filled_of(job) if s % 2 else first_of_pair, 1)

            def one_tile(c, dst, a_hi, a_lo, k_tiles, tile):
                cols = slice(P * tile, P * tile + P)
                hi, lo = weights(c, chunk_width(c) // k_tiles)
                for k in range(k_tiles):
                    pe.matmul(dst, hi[:, k, cols], a_lo[:, k, :], start=k == 0, stop=False)
                    pe.matmul(dst, hi[:, k, cols], a_hi[:, k, :], start=False, stop=False)
                    last = pe.matmul(dst, lo[:, k, cols], a_hi[:, k, :], start=False, stop=k == k_tiles - 1)
                return last

            def two_tiles(c, job, a_hi, a_lo, k_tiles, first):
                for f in range(2):
                    last = one_tile(c, bank_of(job)[:, 256 * f:256 * f + 256], a_hi, a_lo, k_tiles, first + f)
                last.then_inc(filled_of(job), 1)

            with pe.Fori(0, DEPTH) as l:
                x_transposes(l, "hT", 0)
                for c in range(C_GATE):
                    if CHUNKS[c][0] == "group":
                        group_half(l, c)
                    elif CHUNKS[c][0] == "uq":
                        latent(l, c, "uq", HEADS * MLA_QK, 0, 2)
                    else:
                        latent(l, c, "ukv", HEADS * 2 * MLA_NOPE, 2, 1)
                    if c == 4:
                        wait_group(l, 0)
                        transposes(l, "sq", z_blocks(SQ))
                        pe.wait_ge(roped, l * ROPES + ONE + 1)
                        transposes(l, "ik", [lambda tt: ik_rep[:, tt, :, :].rearrange("p r d -> p (r d)")])
                    if c == 6:
                        pe.wait_ge(normed_ready, l * NORMED + 6)
                        transposes(l, "ckv", [lambda tt: c_norm[:, tt, MLA_Q:MLA_Q + MLA_KV]])
                    if c == 8:
                        wait_group(l, 3)
                        transposes(l, "sk", z_blocks(SK))
                        pe.wait_ge(normed_ready, l * NORMED + 8)
                        transposes(l, "cq", [lambda tt, a=P * k: c_norm[:, tt, a:a + P] for k in range(2)])
                    if c == 12:
                        pe.wait_ge(roped, l * ROPES + ONE + 3)
                        transposes(l, "iq", z_blocks(IQ))
                    if c == 14:
                        pe.wait_ge(roped, l * ROPES + ONE + 4)
                        transposes(l, "mq", z_blocks(MQ))
                        transposes(l, "mk", z_blocks(MK))
                pe.wait_ge(roped, l * ROPES + ONE + 5)
                for tt in range(TT):
                    wait_drained(pe, l, ("ukv", tt))
                for name, cat in (("mlaq", q_cat), ("mlak", k_cat)):
                    for h in range(2):
                        transposes(l, f"{name}{h}", [lambda tt, a=MLA_QK * (2 * h + k), c=cat: c[:, tt, a:a + MLA_QK]
                                                     for k in range(2)])
                index_products(l)
                pe.wait_ge(roped, l * ROPES + ONE + 6)
                transposes(l, "dq", z_blocks(DQ))
                transposes(l, "dk", z_blocks(DK))
                for s in range(16):
                    head_logits(l, s)
                    wait_chunk(l, C_GATE + s)
                    wait_empty(pe, l, ("gate", s))
                    two_tiles(C_GATE + s, ("gate", s), aT_hi, aT_lo, KT, 0)
                    head_turn(l, s)
                    if s >= 1:
                        head_values(l, s - 1)
                for n in range(N_BRANCH):
                    wait_chunk(l, C_BRANCH + n)
                    wait_drained(pe, l, ("O", 2 * n + 1))
                    for q in range(4):
                        job = ("proj", n, q)
                        wait_empty(pe, l, job)
                        two_tiles(C_BRANCH + n, job, oT_hi[:, 2 * n:2 * n + 2, :], oT_lo[:, 2 * n:2 * n + 2, :], 2, 2 * q)
                    if n == 0:
                        head_values(l, 15)
                for c in range(C_OUT, C_MLP):
                    _, half, kh = CHUNKS[c]
                    hi, lo = weights(c, 512)
                    wait_chunk(l, c)
                    if kh == 0:
                        for tt in range(TT):
                            wait_empty(pe, l, ("out", half, tt))
                    order = [(tt, kk) for kk in range(4) for tt in range(TT)]
                    if (half, kh) == (1, 1):
                        order.sort()
                    for tt, kk in order:
                        job, k, t = ("out", half, tt), 4 * kh + kk, slice(P * tt, P * tt + P)
                        if half == 0 and tt == 0 and k % 2 == 0:
                            pe.wait_ge(merged_lo_ready, l * 4 + k // 2 + 1)
                        last = products(bank_of(job)[:, :], aT_hi[:, k, t], aT_lo[:, k, t],
                                        hi[:, kk, :], lo[:, kk, :], k == 0, k == KT - 1)
                        if k == KT - 1:
                            last.then_inc(filled_of(job), 1)
                    if kh == 0:
                        last.then_inc(chunk_used, 1)
                x_transposes(l, "h2T", 8)
                def up(j, i=None):
                    more = 0 if i is None else i
                    c = C_MLP if j == 0 else C_MLP - 1 + 2 * j
                    wait_chunk(l, c, i)
                    wait_empty(pe, l, ("up", j), more)
                    if j == 0:
                        for tt in range(TT):
                            for q in (2 * tt, 2 * tt + 1):
                                wait_drained(pe, l, ("h2T", q))
                            t = slice(P * tt, P * tt + P)
                            one_tile(c, bank_of(("up", 0))[:, t], aT_hi[:, :, t], aT_lo[:, :, t], KT, 0)
                        one_tile(c, bank_of(("up", 0))[:, 256:512], aT_hi, aT_lo, KT, 1)\
                            .then_inc(filled_of(("up", 0)), 1)
                        return
                    two_tiles(c, ("up", j), aT_hi, aT_lo, KT, 0)

                def down(j, i=None):
                    more = 0 if i is None else i
                    c = C_MLP + 2 + 2 * j if j < FF_STEPS - 1 else NCH - 1
                    hi, lo = weights(c, D_MODEL)
                    wait_chunk(l, c, i)
                    pe.wait_ge(u_lo_ready, l * FF_STEPS + j + 1 + 3 * more)
                    for tt in range(TT):
                        for half in range(2):
                            job = ("down", tt, half)
                            for k in range(2):
                                t = slice(256 * k + P * tt, 256 * k + P * tt + P)
                                cols = slice(512 * half, 512 * half + 512)
                                start = j == 0 and k == 0
                                last = products(bank_of(job)[:, :], uT_hi[:, j % 3, t], uT_lo[:, j % 3, t],
                                                hi[:, k, cols], lo[:, k, cols], start,
                                                j == FF_STEPS - 1 and k == 1)
                            if j == FF_STEPS - 1:
                                last.then_inc(filled_of(job), 1)
                    if j < FF_STEPS - 1:
                        last.then_inc(chunk_used, 1)
                    return last

                up(0)
                up(1)
                down(0)
                with pe.Fori(0, 4) as i:
                    for j in (1, 2, 3):
                        up(j + 1, i)
                        down(j, i)
                for j in (13, 14):
                    up(j + 1)
                    down(j)
                down(15)


_SHAPES = ["x", "w_small", "w_big", "gains", "gate_bias", "consts"]


def kernel(**inputs):
    import numpy as np
    import concourse.bacc as bacc
    from concourse.bass_utils import run_bass_kernel_spmd

    w = {k: np.asarray(v) for k, v in inputs.items()}
    f32 = np.float32

    def tiles(a):
        return a.reshape(-1, P, a.shape[1]).transpose(1, 0, 2).reshape(P, -1)

    w_small = np.empty((DEPTH, SMALL_AT[-1]), f32)
    w_big = np.empty((DEPTH, NCH - C_GATE, P, CW), f32)
    for l in range(DEPTH):
        for c, (kind, *n) in enumerate(CHUNKS):
            if kind == "group":
                first, width = GROUPS[n[0]]
                a = w["w_in"][l, 512 * n[1]:512 * n[1] + 512, first:first + width]
            elif kind == "uq":
                a = w["w_uq"][l]
            elif kind == "ukv":
                a = w["w_ukv"][l]
            elif kind == "gate":
                a = w["w_in"][l, :, GATE0 + 256 * n[0]:GATE0 + 256 * n[0] + 256]
            elif kind == "branch":
                a = w["w_branch"][l, PROJ_ORDER[n[0]]]
            elif kind == "out":
                a = w["w_out"][l, 512 * n[1]:512 * n[1] + 512, 512 * n[0]:512 * n[0] + 512]
            elif kind == "up":
                a = w["w_up"][l, :, 256 * n[0]:256 * n[0] + 256]
            else:
                a = w["w_down"][l, 256 * n[0]:256 * n[0] + 256, :]
            if c < C_GATE:
                w_small[l, SMALL_AT[c]:SMALL_AT[c + 1]] = tiles(a).ravel()
            else:
                w_big[l, c - C_GATE] = tiles(a)

    gains = np.empty((DEPTH + 1, GAIN_W), f32)
    bias = np.empty((DEPTH + 1, P, 32), f32)
    for l in range(DEPTH + 1):
        n = min(l, DEPTH - 1)
        gains[l, GAIN_MIX:GAIN_MLP] = w["norm_mix"][n] if l < DEPTH else w["norm_final"]
        gains[l, GAIN_MLP:GAIN_Q] = w["norm_mlp"][n]
        gains[l, GAIN_Q:GAIN_KV] = w["mla_q_norm"][n]
        gains[l, GAIN_KV:GAIN_W] = w["mla_kv_norm"][n]
        bias[l] = w["b_gate"][n].reshape(32, P).T

    consts = np.zeros((P, CONST_W), f32)
    r = np.arange(P)

    def put(name, a):
        consts[:, CONST_AT[name]:CONST_AT[name] + CONSTS[name]] = a

    put("ident", r[:, None] == r[None, :])
    put("negsuf", -(r[:, None] >= r[None, :]).astype(f32))
    put("negones", -1.0)
    put("causal", np.where(r[None, :] > r[:, None], NEG, 0.0))
    put("past", np.where(r[:, None] >= r[None, :], NEG, 0.0))
    tables = []
    for n_rot in (HEAD_DIM // 4, IDX_DIM // 4, MLA_ROPE):
        inv = (1.0 / (ROPE_THETA ** (np.arange(0, n_rot, 2, dtype=f32) / f32(n_rot)))).astype(f32)
        ang = (np.arange(SEQ, dtype=f32)[:, None] * inv[None, :]).astype(f32)
        tables += [np.cos(ang), np.sin(ang)]
    table = np.concatenate(tables, axis=1).astype(f32)
    put("rope", table.reshape(TT, P, 56).transpose(1, 0, 2).reshape(P, TT * 56))
    put("num", np.array([NORM_EPS, -0.5], f32)[None, :])

    nc = bacc.Bacc("TRN2", target_bir_lowering=False, num_devices=1)
    arrays, args = {}, []
    for name, a in zip(_SHAPES, (w["x"], w_small, w_big, gains, bias, consts)):
        arrays[name] = np.ascontiguousarray(a)
        args.append(nc.dram_tensor(name, a.shape, mybir.dt.from_np(a.dtype), kind="ExternalInput").ap())
    args.append(nc.dram_tensor("out", (1, SEQ, D_MODEL), mybir.dt.float32, kind="ExternalOutput").ap())
    build(nc, *args)
    result = run_bass_kernel_spmd(nc, [arrays], core_ids=[0])
    return result.results[0]["out"]
```

```python
from contextlib import ExitStack

import concourse.bass as bass
from concourse import mybir

DEPTH, SEQ, D_MODEL, D_FF = 2, 256, 1024, 4096
P = 128
TT = SEQ // P
KT = D_MODEL // P
HEAD_DIM, N_BRANCH, HEADS = 64, 4, 4
IDX_HEADS, IDX_DIM, IDX_TOP = 8, 32, SEQ // 4
MLA_Q, MLA_KV, MLA_NOPE, MLA_ROPE = 256, 128, 64, 32
MLA_QK = MLA_NOPE + MLA_ROPE
NORM_EPS, ROPE_THETA = 1e-6, 500000.0
BW = HEADS * HEAD_DIM
GATE0 = 3016

GROUPS = [((1024, 296), (2856, 160)), ((2344, 512),), ((1320, 512),), ((512, 512),), ((1832, 512),), ((0, 512),)]
GROUP_W = [sum(w for _, w in parts) for parts in GROUPS]
IK, IW, SQ, CKV, KR, CQ, SK, IQ, MQ, MK, DQ, DK, ZW = 0, 32, 40, 296, 424, 456, 712, 968, 1224, 1480, 1736, 1992, 2248

QUARTERS = 4
CHUNKS = [("group", 0, quarter) for quarter in range(QUARTERS)]
CHUNKS += [("group", g, half) for g in range(1, 5) for half in range(2)] + [("uq",), ("ukv",)]
CHUNKS += [("group", 5, 0), ("group", 5, 1)]
CHUNKS += [("gate", j) for j in range(16)]
PROJ_ORDER = [1, 2, 3, 0]
CHUNKS += [("branch", n) for n in range(N_BRANCH)]
CHUNKS += [("out", half, kh) for half in range(2) for kh in range(2)]
CHUNKS += [("up", 0)] + [x for j in range(15) for x in (("up", j + 1), ("down", j))] + [("down", 15)]
NCH = len(CHUNKS)
CW = 2048
C_GATE, C_BRANCH, C_OUT, C_MLP = 16, 32, 36, 40
RING = 3
FF_STEPS = D_FF // 256


def parts_of(g):
    return QUARTERS if g == 0 else 2


def chunk_width(c):
    kind = CHUNKS[c]
    if kind[0] == "group":
        return GROUP_W[kind[1]] * KT // parts_of(kind[1])
    return {"uq": 2 * HEADS * MLA_QK, "ukv": HEADS * 2 * MLA_NOPE}.get(kind[0], CW)


SMALL_AT = [0]
for _c in range(C_GATE):
    SMALL_AT.append(SMALL_AT[-1] + P * chunk_width(_c))

CONSTS = dict(ident=128, negsuf=128, negones=128, causal=128, past=128, rope=TT * 56, num=3)
CONST_AT, CONST_W = {}, 0
for _n, _w in CONSTS.items():
    CONST_AT[_n] = CONST_W
    CONST_W += _w
NEG, TAKEN = -1.0e30, -3.0e38
GAIN_MIX, GAIN_MLP, GAIN_Q, GAIN_KV, GAIN_W = 0, 1024, 2048, 2304, 2432


def psum_plan():
    jobs, fills = {}, [0] * 8

    def add(job, bank):
        jobs[job] = (bank, fills[bank])
        fills[bank] += 1

    stream = [("hT", q) for q in range(4)]
    for g in range(5):
        stream += [("group", g, 0), ("group", g, 1)]
    stream += [("uq", 0), ("uq", 1), ("ukv", 0), ("ukv", 1), ("group", 5, 0), ("group", 5, 1)]
    stream += [("gate", j) for j in range(16)]
    stream += [("proj", n, q) for n in range(N_BRANCH) for q in range(4)]
    stream += [("out", half, tt) for half in range(2) for tt in range(TT)]
    stream += [("h2T", q) for q in range(4)]
    stream += [("utok", tt, j) for tt in range(TT) for j in range(2)]
    for n, job in enumerate(stream):
        add(job, n % 4)
    for j in range(FF_STEPS):
        add(("up", j), j % 3)
    for tt in range(TT):
        for half in range(2):
            add(("down", tt, half), 4 + 2 * tt + half)
    for n, name in enumerate(["sq", "ik", "ckv", "sk", "cq", "iq"]):
        add(("T", name), 4 + n % 4)
    for qt in (1, 0):
        for r in range(4):
            add(("idx", qt, r), 4 + r)
    for name, b in dict(mq=4, mk=5, mlaq0=6, mlaq1=7, mlak0=6, mlak1=7, dq=6, dk=7).items():
        add(("T", name), b)
    for s in range(16):
        add(("S", s), 4 + s % 2)
        if s >= 4:
            add(("PT", s), 6)
        if s % 2:
            add(("O", s // 2), 7)
    return jobs, fills


JOBS, FILLS = psum_plan()


def used_plan():
    plan, count = [], 0
    for kind in CHUNKS:
        fills = {"group": ("group", *kind[1:2], 1), "uq": ("uq", 1), "ukv": ("ukv", 1), "gate": kind,
                 "branch": ("proj", kind[-1], 3), "out": ("out", *kind[1:2], 1),
                 "up": ("utok", 1, kind[-1]) if kind[-1] in (0, 1) else kind}.get(kind[0])
        last_part = parts_of(kind[1]) - 1 if kind[0] == "group" else 1
        if fills is None or (kind[0] in ("group", "out") and kind[2] < last_part):
            count += kind != ("down", FF_STEPS - 1)
            plan.append([None, count, None])
        else:
            b, turn = JOBS[fills]
            plan.append([b, turn + 1, FILLS[b]])
    return [(b, n, count if b is None else per) for b, n, per in plan], count


USED_BY, CHUNKS_USED = used_plan()

SQUARES, NORMED = 12, 12
NORMS, ROPES, POOL_LINKS, ACT_LINKS = 8, 6, 6 + 2 * 4 + 4, 8


def build(nc, x, w_small, w_big, gains, gate_bias, consts, out):
    F32, F32R, BF16 = mybir.dt.float32, mybir.dt.float32r, mybir.dt.bfloat16
    ALU, ACT, AX = mybir.AluOpType, mybir.ActivationFunctionType, mybir.AxisListType
    ctx = ExitStack()
    with ctx:
        def sb(name, shape, dt=F32, where=ctx):
            return where.enter_context(nc.sbuf_tensor(name, shape, dt))

        def sem(name):
            return ctx.enter_context(nc.semaphore(name))

        x_sb = sb("x_sb", [P, TT, D_MODEL])
        gain = sb("gain", [P, GAIN_W])
        bias = sb("bias", [P, 32])
        cst = sb("cst", [P, CONST_W])
        ident_bf = sb("ident_bf", [P, P], BF16)
        causal_bf = sb("causal_bf", [P, P], BF16)
        past_bf = sb("past_bf", [P, P], BF16)
        stage = sb("stage", [P, RING, CW])
        w_hi = sb("w_hi", [P, RING, CW], F32R)
        w_lo = sb("w_lo", [P, RING, CW], F32R)
        aT_hi = sb("aT_hi", [P, KT, SEQ], F32R)
        aT_lo = sb("aT_lo", [P, KT, SEQ], F32R)
        sumsq = sb("sumsq", [P, NORMS, 2])
        mean = sb("mean", [P, 2, NORMS])
        rstd = sb("rstd", [P, NORMS])
        values = sb("values", [P, TT, 3, BW])
        v_mla = sb("v_mla", [P, TT, BW])
        mla_qT = sb("mla_qT", [P, HEADS, SEQ])
        mla_kT = sb("mla_kT", [P, HEADS, SEQ])
        probs = sb("probs", [P, 2, 384])
        probsT = sb("probsT", [P, 2, 384])
        rowmax = sb("rowmax", [P, 2, 2])
        negmax = sb("negmax", [P, 2, 2])
        rowsum = sb("rowsum", [P, 2, 2])
        rowinv = sb("rowinv", [P, 2, 2])
        oT_hi = sb("oT_hi", [P, 8, SEQ], F32R)
        oT_lo = sb("oT_lo", [P, 8, SEQ], F32R)
        rel = sb("rel", [P, 2, 512])
        score = [sb(f"score{n}", [P, 384]) for n in range(2)]
        top8 = sb("top8", [P, 2, 8])
        idx_w = sb("idx_w", [P, TT, IDX_HEADS])
        dsa_mask = sb("dsa_mask", [P, 384], BF16)
        rope_tmp = sb("rope_tmp", [P, 4, 128])
        qk_region = sb("qk_region", [P, 15 * 256])

        def piece(n, blocks=2):
            return qk_region[:, 512 * n:512 * n + 256 * blocks].rearrange("p (b t) -> p b t", t=SEQ)

        sqT, skT, mqT, mkT, dqT, dkT, iqT = (piece(n) for n in range(7))
        ikT = qk_region[:, 14 * 256:15 * 256]
        merged = qk_region[:, 0:2048].rearrange("p (f t) -> p f t", t=SEQ)
        product = qk_region[:, 2048:3584].rearrange("p (a n) -> p a n", a=3)
        junk = [qk_region[:, D_MODEL * t:D_MODEL * t + D_MODEL] for t in range(TT)]
        small_junk = [qk_region[:, 2048 + 256 * n:2304 + 256 * n] for n in range(4)]
        with ExitStack() as first:
            zq = sb("zq", [P, TT, ZW], where=first)
            q_cat = sb("q_cat", [P, TT, HEADS * MLA_QK], where=first)
            k_cat = sb("k_cat", [P, TT, HEADS * MLA_QK], where=first)
            c_norm = sb("c_norm", [P, TT, 384], where=first)
            ik_rep = sb("ik_rep", [P, TT, 4, IDX_DIM], where=first)
            cT_hi = sb("cT_hi", [P, 3, SEQ], F32R, where=first)
            cT_lo = sb("cT_lo", [P, 3, SEQ], F32R, where=first)
        with ExitStack() as second:
            gates = sb("gates", [P, 16, 512], where=second)
        with ExitStack() as third:
            xn = sb("xn", [P, TT, D_MODEL], where=third)
            act_sq = sb("act_sq", [P, 3, 512], where=third)
            uT_hi = sb("uT_hi", [P, 3, 512], F32R, where=third)
            uT_lo = sb("uT_lo", [P, 3, 512], F32R, where=third)

        bank = [ctx.enter_context(nc.psum_tensor(f"bank{n}", [P, 512], F32)) for n in range(8)]

        def const(name, a=0, b=None):
            at = CONST_AT[name]
            return cst[:, at + a:at + (CONSTS[name] if b is None else b)]

        ident, negsuf, negones, causal = (const(n) for n in ("ident", "negsuf", "negones", "causal"))
        rope_tab = const("rope").rearrange("p (t n) -> p t n", t=TT)

        loaded = [sem(f"loaded{n}") for n in range(RING)]
        x_loaded, consts_loaded = [sem(f"x_loaded{tt}") for tt in range(TT)], sem("consts_loaded")
        mix_loaded = sem("mix_loaded")
        gains_loaded = sem("gains_loaded")
        hi_ready = sem("hi_ready")
        lo_ready = sem("lo_ready")
        chunk_used = sem("chunk_used")
        filled = [sem(f"filled{n}") for n in range(8)]
        drained = [sem(f"drained{n}") for n in range(8)]
        squares_ready = sem("squares_ready")
        rstd_ready = sem("rstd_ready")
        normed_ready = sem("normed_ready")
        a_hi_ready = sem("a_hi_ready")
        merged_lo_ready = sem("merged_lo_ready")
        c_hi_ready = sem("c_hi_ready")
        roped = sem("roped")
        pool_link, act_link, dve_link = sem("pool_link"), sem("act_link"), sem("dve_link")
        rel_used = sem("rel_used")
        mask_ready = sem("mask_ready")
        ln_ready = sem("ln_ready")
        negmax_ready = sem("negmax_ready")
        probs_ready = sem("probs_ready")
        cum_done = sem("cum_done")
        first_of_pair = sem("first_of_pair")
        o_hi_ready = sem("o_hi_ready")
        gates_ready = sem("gates_ready")
        pool_sums = sem("pool_sums")
        merged_ready = sem("merged_ready")
        relu_ready = sem("relu_ready")
        tok_relu_ready = sem("tok_relu_ready")
        u_hi_ready, u_lo_ready = sem("u_hi_ready"), sem("u_lo_ready")
        const_ready = sem("const_ready")
        stored = sem("stored")

        ONE = 1

        def wait_filled(e, l, job, more=0):
            b, turn = JOBS[job]
            e.wait_ge(filled[b], l * FILLS[b] + ONE + turn + 1 + more)

        def wait_drained(e, l, job, more=0):
            b, turn = JOBS[job]
            e.wait_ge(drained[b], l * FILLS[b] + ONE + turn + 1 + more)

        def wait_empty(e, l, job, more=0):
            b, turn = JOBS[job]
            e.wait_ge(drained[b], l * FILLS[b] + ONE + turn + more)

        def wait_read(e, l, jobs, empty=None):
            need = {}
            for job in jobs:
                b, turn = JOBS[job]
                need[b] = max(need.get(b, 0), turn + 1)
            if empty is not None:
                b, turn = JOBS[empty]
                need[b] = max(need.get(b, 0), turn)
            for b, turn in need.items():
                e.wait_ge(drained[b], l * FILLS[b] + ONE + turn)

        def wait_chunk_used(e, l, c, more=0):
            if CHUNKS[c][0] == "down" and CHUNKS[c][1] == FF_STEPS - 1:
                wait_filled(e, l, ("down", 1, 1))
                return
            signal, count, per_layer = USED_BY[c % NCH]
            e.wait_ge(chunk_used if signal is None else filled[signal],
                      l * per_layer + ONE + count - (per_layer if c < 0 else 0) + more)

        def wait_head_done(e, l, s):
            if s % 2:
                wait_filled(e, l, ("O", s // 2))
            else:
                e.wait_ge(first_of_pair, l * 8 + s // 2 + 1)

        def bank_of(job):
            return bank[JOBS[job][0]]

        def filled_of(job):
            return filled[JOBS[job][0]]

        def drained_of(job):
            return drained[JOBS[job][0]]

        def four(b):
            return b[:, :].rearrange("p (a t) -> p a t", t=P)

        def a_tiles(aT, q):
            return aT[:, 4 * (q % 2):4 * (q % 2) + 4, P * (q // 2):P * (q // 2) + P]

        def two(ap):
            return ap.rearrange("p (a t) -> p a t", t=SEQ)

        SB_KIND, MOBA_KIND, MLA_KIND, DSA_KIND = range(4)

        def head_scale(s):
            return float(MLA_QK) ** -0.5 if s // 4 == MLA_KIND else 1.0

        def group_pieces(g, tt, b):
            if g == 0:
                rep = b[:, 8:IDX_DIM].unsqueeze(1).to_broadcast([P, 4, IDX_DIM - 8])
                return [(ik_rep[:, tt, :, 8:IDX_DIM], rep), (zq[:, tt, IK:IK + GROUP_W[0]], b[:, 0:GROUP_W[0]])]
            if g in (4, 5):
                at = MQ if g == 4 else DQ
                return [(zq[:, tt, at:at + 512], b[:, :])]
            v, at, first = {1: (1, CQ, True), 2: (0, SK, False), 3: (2, IQ, True)}[g]
            a, c = (0, 256) if first else (256, 0)
            return [(values[:, tt, v, :], b[:, a:a + 256]), (zq[:, tt, at:at + 256], b[:, c:c + 256])]

        def evac_uq(e, l, tt):
            job = ("uq", tt)
            wait_filled(e, l, job)
            if tt == 0:
                e.activation(q_cat[:, tt, :], bank_of(job)[:, 0:384], ACT.Copy).then_inc(drained_of(job), 1)
            else:
                e.tensor_copy(q_cat[:, tt, :], bank_of(job)[:, 0:384]).then_inc(drained_of(job), 1)

        def evac_ukv(e, l, tt):
            job = ("ukv", tt)
            wait_filled(e, l, job)
            kv = bank_of(job)[:, :].rearrange("p (h d) -> p h d", h=HEADS)
            k_to = k_cat[:, tt, :].rearrange("p (h d) -> p h d", h=HEADS)[:, :, 0:MLA_NOPE]
            v_to = v_mla[:, tt, :].rearrange("p (h d) -> p h d", h=HEADS)
            if tt == 0:
                e.activation(k_to, kv[:, :, 0:MLA_NOPE], ACT.Copy)
                e.activation(v_to, kv[:, :, MLA_NOPE:128], ACT.Copy).then_inc(drained_of(job), 1)
            else:
                e.tensor_copy(k_to, kv[:, :, 0:MLA_NOPE])
                e.tensor_copy(v_to, kv[:, :, MLA_NOPE:128]).then_inc(drained_of(job), 1)

        block = ctx.enter_context(nc.Block())

        @block.sync
        def _(sp):
            def load(l, c):
                sp.wait_ge(lo_ready, l * NCH + c + 1)
                if c < C_GATE:
                    n = chunk_width(c)
                    src = w_small[l, SMALL_AT[c]:SMALL_AT[c + 1]].rearrange("(p n) -> p n", n=n)
                    sp.dma_start(stage[:, c % RING, 0:n], src).then_inc(loaded[c % RING], 16)
                else:
                    sp.dma_start(stage[:, c % RING, :], w_big[l, c - C_GATE, :, :]).then_inc(loaded[c % RING], 16)

            def load_mix_gain(l):
                sp.dma_start(gain[:, 0:GAIN_MLP], gains[l, 0:GAIN_MLP].partition_broadcast(P)).then_inc(mix_loaded, 16)

            def load_gains(l):
                sp.dma_start(gain[:, GAIN_MLP:], gains[l, GAIN_MLP:].partition_broadcast(P)).then_inc(gains_loaded, 16)
                sp.dma_start(bias[:, :], gate_bias[l, :, :]).then_inc(gains_loaded, 16)

            with sp.Fori(0, DEPTH) as l:
                for c in range(2):
                    load(l, c)
                sp.wait_ge(x_loaded[0], 16)
                for c in range(2, 4):
                    load(l, c)
                sp.wait_ge(normed_ready, l * NORMED + 2)
                load_gains(l)
                for c in range(4, C_MLP + 3):
                    load(l, c)
                with sp.Fori(0, 4) as i:
                    for c in range(C_MLP + 3, C_MLP + 9):
                        sp.wait_ge(lo_ready, l * NCH + i * 6 + c + 1)
                        sp.dma_start(stage[:, c % RING, :], w_big[l, i * 6 + (c - C_GATE), :, :])\
                          .then_inc(loaded[c % RING], 16)
                for c in range(C_MLP + 27, NCH):
                    load(l, c)
                sp.wait_ge(normed_ready, l * NORMED + 4)
                load_mix_gain(l + 1)
            for tt in range(TT):
                sp.wait_ge(normed_ready, DEPTH * NORMED + 2 * tt + 2)
                sp.dma_start(out[0, P * tt:P * tt + P, :], xn[:, tt, :]).then_inc(stored, 16)
            sp.wait_ge(stored, 16 * TT)

        @block.gpsimd
        def _(pool):
            pool.wait_ge(consts_loaded, 16)
            def norm_factor(l, n, later=0):
                halves = n in (0, 1, 6, 7)
                squares = {0: 1, 1: 3, 2: 5, 3: 6, 4: 7, 5: 8, 6: 9, 7: 11}[n]
                squares += SQUARES * later
                pool.wait_ge(squares_ready, l * SQUARES + squares)
                links = NORM_LINK[n] + POOL_LINKS * later
                pool.tensor_tensor(mean[:, 0, n:n + 1], sumsq[:, n, 0:1], const("num", 0, 1), ALU.add)\
                    .then_inc(pool_link, 1)
                pool.wait_ge(pool_link, l * POOL_LINKS + links + 1)
                if halves:
                    pool.wait_ge(squares_ready, l * SQUARES + squares + 1)
                    pool.tensor_tensor(mean[:, 1, n:n + 1], mean[:, 0, n:n + 1], sumsq[:, n, 1:2], ALU.add)\
                        .then_inc(pool_link, 1)
                    pool.wait_ge(pool_link, l * POOL_LINKS + links + 2)
                pool.tensor_tensor(rstd[:, n:n + 1], mean[:, 1 if halves else 0, n:n + 1], const("num", 1, 2), ALU.pow)\
                    .then_inc(rstd_ready, 1)

            NORM_LINK = {0: 0, 1: 2, 2: 6, 3: 7, 4: 8, 5: 9, 6: 14, 7: 16}
            ROPE_LINK = {"ik": 4, "kr": 5, "iq": 10, "m": 11, "mlaq": 12, "d": 13}

            def rope(l, name, src, heads, half, tab, dst=None, copies=1):
                x1, x2 = src[:, :, :, 0:half], src[:, :, :, half:2 * half]
                cos = rope_tab[:, :, tab:tab + half].unsqueeze(2).to_broadcast([P, TT, heads, half])
                sin = rope_tab[:, :, tab + half:tab + 2 * half].unsqueeze(2).to_broadcast([P, TT, heads, half])
                n = TT * heads * half
                tmp = [rope_tmp[:, k, 0:n].rearrange("p (t h d) -> p t h d", t=TT, h=heads) for k in range(4)]
                pool.wait_ge(roped, l * ROPES + ONE + list(ROPE_LINK).index(name))
                pool.tensor_tensor(tmp[0], x1, cos, ALU.mult)
                pool.tensor_tensor(tmp[1], x2, sin, ALU.mult)
                pool.tensor_tensor(tmp[2], x2, cos, ALU.mult)
                pool.tensor_tensor(tmp[3], x1, sin, ALU.mult).then_inc(pool_link, 1)
                pool.wait_ge(pool_link, l * POOL_LINKS + ROPE_LINK[name] + 1)
                if copies > 1:
                    tmp = [t.to_broadcast([P, TT, copies, half]) for t in tmp]
                d = src if dst is None else dst
                pool.tensor_tensor(d[:, :, :, 0:half], tmp[0], tmp[1], ALU.subtract)
                pool.tensor_tensor(d[:, :, :, half:2 * half], tmp[2], tmp[3], ALU.add).then_inc(roped, 1)

            def group_there(l, g):
                for tt in range(TT):
                    wait_drained(pool, l, (*g, tt))

            def heads_of(a, n, dim):
                return zq[:, :, a:a + n * dim].rearrange("p t (h d) -> p t h d", d=dim)

            for tt in range(TT):
                norm_factor(0, tt)
            one = const("num", 2, 3).to_broadcast([P, P])
            pool.tensor_tensor(ident_bf[:, :], ident, one, ALU.mult)
            pool.tensor_tensor(causal_bf[:, :], causal, one, ALU.mult)
            pool.tensor_tensor(past_bf[:, :], const("past"), one, ALU.mult).then_inc(const_ready, 1)

            with pool.Fori(0, DEPTH) as l:
                group_there(l, ("group", 0))
                rope(l, "ik", heads_of(IK, 1, IDX_DIM), 1, 4, 16, dst=ik_rep, copies=4)
                rope(l, "kr", heads_of(KR, 1, MLA_ROPE), 1, 16, 24,
                     dst=k_cat[:, :, :].rearrange("p t (h d) -> p t h d", h=HEADS)[:, :, :, MLA_NOPE:MLA_QK], copies=4)
                for n in (2, 3):
                    norm_factor(l, n)
                for n in (4, 5):
                    norm_factor(l, n)
                group_there(l, ("group", 3))
                rope(l, "iq", heads_of(IQ, IDX_HEADS, IDX_DIM), IDX_HEADS, 4, 16)
                group_there(l, ("group", 4))
                rope(l, "m", heads_of(MQ, 8, HEAD_DIM), 8, 8, 0)
                group_there(l, ("uq",))
                rope(l, "mlaq", q_cat[:, :, :].rearrange("p t (h d) -> p t h d", h=HEADS)[:, :, :, MLA_NOPE:MLA_QK],
                     HEADS, 16, 24)
                group_there(l, ("group", 5))
                rope(l, "d", heads_of(DQ, 8, HEAD_DIM), 8, 8, 0)
                for k in range(8):
                    wait_drained(pool, l, ("proj", 1 + k // 4, k % 4))
                    if k >= 4:
                        pool.wait_ge(pool_sums, l * 8 + k - 3)
                    m = qk_region[:, 512 * (k % 4):512 * (k % 4) + 512]
                    pool.tensor_tensor(m, m, product[:, k % 3, :], ALU.add).then_inc(pool_sums, 1)
                pool.wait_ge(hi_ready, l * NCH + C_OUT + 2)
                pool.wait_ge(lo_ready, l * NCH + RING + C_OUT + 1)
                slot = (C_OUT + 1) % RING
                pool.tensor_tensor(w_lo[:, slot, :], stage[:, slot, :], w_hi[:, slot, :].bitcast(F32), ALU.subtract)\
                    .then_inc(lo_ready, 1)
                for n in (6, 7):
                    norm_factor(l, n)
                for n in (0, 1):
                    norm_factor(l, n, later=1)

        @block.scalar
        def _(act):

            def split_hi(l, c, i=None):
                n, more = (chunk_width(c), 0) if i is None else (CW, i * (1 if CHUNKS[c - RING][0] == "up" else 3))
                act.wait_ge(loaded[c % RING], (l * (NCH // RING) + c // RING + 1 + (0 if i is None else i * 2)) * 16)
                wait_chunk_used(act, l, c - RING, more)
                act.activation(w_hi[:, c % RING, 0:n], stage[:, c % RING, 0:n], ACT.Copy).then_inc(hi_ready, 1)

            def x_squares(l, n, after):
                for half in range(2):
                    wait_drained(act, l, after(n % 2, half))
                    cols = slice(512 * half, 512 * half + 512)
                    act.activation(junk[n % 2][:, cols], x_sb[:, n % 2, cols], ACT.Square, scale=D_MODEL ** -0.5,
                                   accum_out=sumsq[:, n, half:half + 1]).then_inc(squares_ready, 1)

            def c_squares(l, n, tt, at, width):
                wait_drained(act, l, ("group", 0 if at == CKV else 1, tt))
                act.activation(small_junk[n - 2][:, 0:width], zq[:, tt, at:at + width], ACT.Square,
                               scale=float(width) ** -0.5, accum_out=sumsq[:, n, 0:1]).then_inc(squares_ready, 1)

            def a_hi(l, name, q):
                job = (name, q)
                wait_filled(act, l, job)
                act.activation(a_tiles(aT_hi, q), four(bank_of(job)), ACT.Copy).then_inc(a_hi_ready, 1)

            def evac_group(l, g):
                job = ("group", g, 0)
                wait_filled(act, l, job)
                b = bank_of(job)
                for k, (dst, src) in enumerate(group_pieces(g, 0, b)):
                    last = act.activation(dst, src, ACT.Copy)
                last.then_inc(drained_of(job), 1)

            def evac_t(l, name, dst, rows=P, scale=1.0):
                job = ("T", name)
                wait_filled(act, l, job)
                act.activation(dst, two(bank_of(job)[0:rows, :]), ACT.Copy, scale=scale).then_inc(drained_of(job), 1)

            def c_hi(l, name, a, n):
                job = ("T", name)
                wait_filled(act, l, job)
                act.activation(cT_hi[:, a:a + n, :], two(bank_of(job)[:, 0:256 * n]), ACT.Copy).then_inc(c_hi_ready, 1)

            def tok_relu(l, tt, j):
                wait_filled(act, l, ("utok", tt, j))
                act.activation(act_sq[:, tt, 256 * j:256 * j + 256], bank_of(("utok", tt, j))[:, 0:256], ACT.Relu)\
                   .then_inc(tok_relu_ready, 1)

            def index_relu(l, qt):
                for r in range(4):
                    job = ("idx", qt, r)
                    n = 4 * (1 - qt) + r
                    wait_filled(act, l, job)
                    if n >= 2:
                        act.wait_ge(rel_used, l * 8 + n - 1)
                    w = 256 * (1 + qt)
                    act.activation(rel[:, n % 2, 0:w], bank_of(job)[:, 0:w], ACT.Relu,
                                   scale=float(IDX_DIM) ** -0.5).then_inc(drained_of(job), 1)

            def head_finish(l, s):
                if s >= 2:
                    wait_head_done(act, l, s - 2)
                if s // 4 == SB_KIND:
                    act.wait_ge(cum_done, l * 4 + s + 1)
                    act.activation(probsT[:, s % 2, :], bank_of(("S", s))[:, 0:384], ACT.Exp)\
                       .then_inc(drained_of(("S", s)), 1)
                else:
                    wait_filled(act, l, ("PT", s))
                    act.activation(probsT[:, s % 2, :], bank_of(("PT", s))[:, 0:384], ACT.Copy)\
                       .then_inc(drained_of(("PT", s)), 1)

            def head_start(l, s):
                S, pr = bank_of(("S", s)), probs[:, s % 2, :]
                if s // 4 == SB_KIND:
                    wait_filled(act, l, ("S", s))
                    act.activation(pr, S[:, 0:384], ACT.Abs).then_inc(act_link, 1)
                    act.wait_ge(act_link, l * ACT_LINKS + 2 * s + 1)
                    act.activation(pr, pr, ACT.Exp, scale=-1.0).then_inc(act_link, 1)
                    act.wait_ge(act_link, l * ACT_LINKS + 2 * s + 2)
                    act.activation(pr, pr, ACT.Ln, bias=1.0).then_inc(ln_ready, 1)
                else:
                    act.wait_ge(negmax_ready, l * 12 + s - 3)
                    for qt, (a, b) in enumerate(((0, 128), (128, 384))):
                        last = act.activation(pr[:, a:b], S[:, a:b], ACT.Exp, bias=negmax[:, s % 2, qt:qt + 1],
                                              scale=head_scale(s), accum_out=rowsum[:, s % 2, qt:qt + 1])
                    last.then_inc(drained_of(("S", s)), 1)

            def gate_logits(l, j):
                job = ("gate", j)
                wait_filled(act, l, job)
                for f in range(2):
                    last = act.activation(gates[:, j, 256 * f:256 * f + 256], bank_of(job)[:, 256 * f:256 * f + 256],
                                          ACT.Identity, bias=bias[:, 2 * j + f:2 * j + f + 1])
                last.then_inc(drained_of(job), 1)

            def sigmoid(l, n):
                b = PROJ_ORDER[n]
                wait_drained(act, l, ("gate", 15))
                act.activation(gates[:, 4 * b:4 * b + 4, :], gates[:, 4 * b:4 * b + 4, :], ACT.Sigmoid)\
                   .then_inc(gates_ready, 1)

            def o_hi(l, p):
                wait_head_done(act, l, 2 * p + 1)
                act.activation(oT_hi[:, p, :], bank_of(("O", p))[:, 0:256], ACT.Copy).then_inc(o_hi_ready, 1)

            act.preload_act_table_set("sigmoid_and_others")
            def load_x(tt):
                act.dma_start(x_sb[:, tt, :], x[0, P * tt:P * tt + P, :]).then_inc(x_loaded[tt], 16)

            load_x(0)
            act.dma_start(cst[:, :], consts).then_inc(consts_loaded, 16)
            act.dma_start(gain[:, 0:GAIN_MLP], gains[0, 0:GAIN_MLP].partition_broadcast(P)).then_inc(mix_loaded, 16)
            load_x(1)
            with act.Fori(0, DEPTH) as l:
                split_hi(l, 0)
                for tt in range(TT):
                    x_squares(l, tt, lambda tt, half: ("down", tt, half))
                    split_hi(l, 1 + tt)
                    for q in (2 * tt, 2 * tt + 1):
                        a_hi(l, "hT", q)
                for c in range(C_GATE):
                    if c == 4:
                        evac_group(l, 0)
                        for tt in range(TT):
                            c_squares(l, 2 + tt, tt, CKV, MLA_KV)
                    if c == 6:
                        evac_t(l, "sq", sqT, scale=0.125)
                        evac_group(l, 1)
                        for tt in range(TT):
                            c_squares(l, 4 + tt, tt, CQ, MLA_Q)
                    if c == 8:
                        c_hi(l, "ckv", 2, 1)
                        evac_group(l, 2)
                    if c == 9:
                        c_hi(l, "cq", 0, 2)
                    if c == 10:
                        evac_group(l, 3)
                    if c == 12:
                        evac_group(l, 4)
                    if c == 13:
                        evac_t(l, "iq", iqT)
                        evac_uq(act, l, 0)
                    if c == 14:
                        evac_ukv(act, l, 0)
                        index_relu(l, 1)
                    if c == 15:
                        index_relu(l, 0)
                    if c >= 1:
                        split_hi(l, c + 2)
                evac_group(l, 5)
                evac_t(l, "mq", mqT, scale=0.125)
                for h in range(2):
                    evac_t(l, f"mlaq{h}", mla_qT[0:MLA_QK, 2 * h:2 * h + 2, :], rows=MLA_QK)
                act.preload_act_table_set("natural_log_exp_and_others")
                for s in range(16):
                    if s >= 1:
                        head_finish(l, s - 1)
                    head_start(l, s)
                    if s == 1:
                        evac_t(l, "dq", dqT, scale=0.125)
                    if s >= 1:
                        gate_logits(l, s - 1)
                    if s >= 3 and s % 2 == 1:
                        o_hi(l, (s - 2) // 2)
                    split_hi(l, C_GATE + s + 2)
                head_finish(l, 15)
                gate_logits(l, 15)
                sigmoid(l, 0)
                split_hi(l, C_BRANCH + 2)
                sigmoid(l, 1)
                o_hi(l, 7)
                split_hi(l, C_BRANCH + 3)
                sigmoid(l, 2)
                split_hi(l, C_BRANCH + 4)
                sigmoid(l, 3)
                split_hi(l, C_BRANCH + 5)
                for q in range(4):
                    act.wait_ge(merged_ready, l * 4 + q + 1)
                    act.activation(aT_hi[:, 2 * q:2 * q + 2, :], merged[:, 2 * q:2 * q + 2, :], ACT.Copy)\
                       .then_inc(a_hi_ready, 1)
                for k in range(3):
                    split_hi(l, C_OUT + k + 2)
                for tt in range(TT):
                    x_squares(l, 6 + tt, lambda tt, half: ("out", half, tt))
                    if tt == 0:
                        split_hi(l, C_MLP + 1)
                    else:
                        tok_relu(l, 0, 0)
                        split_hi(l, C_MLP + 2)
                    for q in (2 * tt, 2 * tt + 1):
                        a_hi(l, "h2T", q)
                tok_relu(l, 0, 1)

                def u_hi(k):
                    wait_filled(act, l, ("up", k))
                    act.activation(uT_hi[:, k, :], bank_of(("up", k))[:, :], ACT.Copy).then_inc(u_hi_ready, 1)

                tok_relu(l, 1, 0)
                u_hi(0)
                tok_relu(l, 1, 1)
                split_hi(l, C_MLP + 3)
                u_hi(1)
                for c in (4, 5, 6):
                    split_hi(l, C_MLP + c)

                def mlp(k, i=None):
                    more = 0 if i is None else i
                    job = ("up", k)
                    wait_filled(act, l, job, more)
                    act.activation(act_sq[:, k % 3, :], bank_of(job)[:, :], ACT.Relu).then_inc(relu_ready, 1)
                    if C_MLP + 3 + 2 * k < NCH:
                        split_hi(l, C_MLP + 3 + 2 * k, i)
                    wait_drained(act, l, job, more)
                    act.activation(uT_hi[:, k % 3, :], act_sq[:, k % 3, :], ACT.Copy).then_inc(u_hi_ready, 1)
                    if C_MLP + 4 + 2 * k < NCH:
                        split_hi(l, C_MLP + 4 + 2 * k, i)

                with act.Fori(0, 4) as i:
                    for k in (2, 3, 4):
                        mlp(k, i)
                for k in (14, 15):
                    mlp(k)
            for tt in range(TT):
                x_squares(DEPTH, tt, lambda tt, half: ("down", tt, half))


        @block.vector
        def _(dve):
            links = [0]

            def link(ins):
                links[0] += 1
                ins.then_inc(dve_link, 1)
                dve.wait_ge(dve_link, links[0])

            dve.sem_inc(lo_ready, RING)
            for count in (*filled, *drained, chunk_used, roped):
                dve.sem_inc(count, ONE)
            for b in range(4, 8):
                dve.memset(bank[b][:, :], 0.0).then_inc(filled[b], 1)
            def split_lo(l, c, i=None):
                n, more = (chunk_width(c), 0) if i is None else (CW, i * 6)
                dve.wait_ge(hi_ready, l * NCH + c + 1 + more)
                dve.tensor_tensor(w_lo[:, c % RING, 0:n], stage[:, c % RING, 0:n],
                                  w_hi[:, c % RING, 0:n].bitcast(F32), ALU.subtract).then_inc(lo_ready, 1)

            def residual(l, tt, half, job):
                wait_filled(dve, l, job)
                dve.wait_ge(x_loaded[tt], 16)
                xs = x_sb[:, tt, 512 * half:512 * half + 512]
                dve.tensor_tensor(xs, bank_of(job)[:, :], xs, ALU.add).then_inc(drained_of(job), 1)

            def x_norm(l, n, gain_at):
                dve.wait_ge(rstd_ready, l * NORMS + n + 1)
                if gain_at == GAIN_MIX:
                    dve.wait_ge(mix_loaded, l * 16 + 16)
                for half in range(2):
                    cols = slice(512 * half, 512 * half + 512)
                    dve.scalar_tensor_tensor(xn[:, n % 2, cols], x_sb[:, n % 2, cols], rstd[:, n:n + 1],
                                             gain[:, gain_at + 512 * half:gain_at + 512 * half + 512],
                                             ALU.mult, ALU.mult).then_inc(normed_ready, 1)

            def tok_square(l, tt, j):
                dve.wait_ge(tok_relu_ready, l * 4 + 2 * tt + j + 1)
                sq = act_sq[:, tt, 256 * j:256 * j + 256]
                dve.scalar_tensor_tensor(sq, bank_of(("utok", tt, j))[:, 0:256], 0.0, sq, ALU.max, ALU.mult)\
                   .then_inc(drained_of(("utok", tt, j)), 1)

            def first_norm(l):
                for half in range(2):
                    residual(l, 0, half, ("down", 0, half))
                split_lo(l, 0)
                x_norm(l, 0, GAIN_MIX)
                split_lo(l, 1)
                residual(l, 1, 0, ("down", 1, 0))
                for q in range(2):
                    a_lo(l, "hT", q, 0)
                residual(l, 1, 1, ("down", 1, 1))
                x_norm(l, 1, GAIN_MIX)
                split_lo(l, 2)
                for q in (2, 3):
                    a_lo(l, "hT", q, 0)

            def second_norm(l):
                for tt, half in ((0, 0), (1, 0), (0, 1)):
                    residual(l, tt, half, ("out", half, tt))
                x_norm(l, 6, GAIN_MLP)
                for q in range(2):
                    a_lo(l, "h2T", q, 8)
                residual(l, 1, 1, ("out", 1, 1))
                split_lo(l, C_MLP + 1)
                x_norm(l, 7, GAIN_MLP)
                tok_square(l, 0, 0)
                for q in (2, 3):
                    a_lo(l, "h2T", q, 8)
                tok_square(l, 0, 1)
                split_lo(l, C_MLP + 2)

            def last_norm():
                for tt in range(TT):
                    for half in range(2):
                        residual(DEPTH, tt, half, ("down", tt, half))
                    x_norm(DEPTH, tt, GAIN_MIX)

            def c_norm_of(l, n, tt, at, to, width, gain_at):
                dve.wait_ge(rstd_ready, l * NORMS + n + 1)
                dve.scalar_tensor_tensor(c_norm[:, tt, to:to + width], zq[:, tt, at:at + width], rstd[:, n:n + 1],
                                         gain[:, gain_at:gain_at + width], ALU.mult, ALU.mult)\
                   .then_inc(normed_ready, 1)

            def a_lo(l, name, q, n):
                job = (name, q)
                dve.wait_ge(a_hi_ready, l * 12 + n + q + 1)
                dve.tensor_tensor(a_tiles(aT_lo, q), four(bank_of(job)), a_tiles(aT_hi, q).bitcast(F32),
                                  ALU.subtract).then_inc(drained_of(job), 1)

            def evac_group(l, g):
                job = ("group", g, 1)
                wait_filled(dve, l, job)
                for dst, src in group_pieces(g, 1, bank_of(job)):
                    last = dve.tensor_copy(dst, src)
                last.then_inc(drained_of(job), 1)

            def evac_t(l, name, dst, rows=P, w=512):
                job = ("T", name)
                wait_filled(dve, l, job)
                src = bank_of(job)[0:rows, 0:w]
                dve.tensor_copy(dst, two(src) if w == 512 else src).then_inc(drained_of(job), 1)

            def c_lo(l, name, a, n):
                job = ("T", name)
                dve.wait_ge(c_hi_ready, l * 2 + (1 if name == "ckv" else 2))
                dve.tensor_tensor(cT_lo[:, a:a + n, :], two(bank_of(job)[:, 0:256 * n]),
                                  cT_hi[:, a:a + n, :].bitcast(F32), ALU.subtract).then_inc(drained_of(job), 1)

            SPAN = {0: (0, 128), 1: (128, 384)}

            def index_scores(l, qt):
                a, b = SPAN[qt]
                w, acc = b - a, score[0][:, a:b]
                for r in range(4):
                    n = 4 * (1 - qt) + r
                    wait_drained(dve, l, ("idx", qt, r))
                    w0, w1 = (idx_w[:, qt, h:h + 1] for h in (r, r + 4))
                    if r == 0:
                        link(dve.tensor_scalar(acc, rel[:, n % 2, 0:w], w0, None, ALU.mult))
                    else:
                        link(dve.scalar_tensor_tensor(acc, rel[:, n % 2, 0:w], w0, acc, ALU.mult, ALU.add))
                    dve.scalar_tensor_tensor(acc, rel[:, n % 2, w:2 * w], w1, acc, ALU.mult, ALU.add)\
                       .then_inc(rel_used, 1)
                    dve.wait_ge(rel_used, l * 8 + n + 1)
                link(dve.tensor_tensor(score[0][:, b - 128:b], score[0][:, b - 128:b], causal, ALU.add))

            def top_round(n):
                for qt in (1, 0):
                    link(dve.max(top8[:, qt, :], score[n % 2][:, slice(*SPAN[qt])]))
                    link(dve.match_replace(score[1 - n % 2][:, slice(*SPAN[qt])], top8[:, qt, :],
                                           score[n % 2][:, slice(*SPAN[qt])], TAKEN))

            def index_mask():
                link(dve.tensor_scalar(score[1][:, :], score[0][:, :], TAKEN, NEG, ALU.not_equal, ALU.mult))
                dve.tensor_copy(dsa_mask[:, 128:256], score[1][:, 128:256])
                dve.tensor_tensor(dsa_mask[:, 0:128], score[1][:, 0:128], causal, ALU.add)
                dve.tensor_tensor(dsa_mask[:, 256:384], score[1][:, 256:384], causal, ALU.add).then_inc(mask_ready, 1)

            def head_max(l, s):
                S = bank_of(("S", s))
                wait_filled(dve, l, ("S", s))
                dve.reduce_max(rowmax[:, s % 2, 0:1], S[:, 0:128], AX.X)
                link(dve.reduce_max(rowmax[:, s % 2, 1:2], S[:, 128:384], AX.X))
                dve.tensor_scalar(negmax[:, s % 2, :], rowmax[:, s % 2, :], -head_scale(s), None, ALU.mult)\
                   .then_inc(negmax_ready, 1)

            def head_norm(l, s):
                wait_drained(dve, l, ("S", s))
                link(dve.reciprocal(rowinv[:, s % 2, :], rowsum[:, s % 2, :]))
                for qt in range(2):
                    a, b = SPAN[qt]
                    last = dve.tensor_scalar(probs[:, s % 2, a:b], probs[:, s % 2, a:b],
                                             rowinv[:, s % 2, qt:qt + 1], None, ALU.mult)
                last.then_inc(probs_ready, 1)

            def softplus(l, s):
                dve.wait_ge(ln_ready, l * 4 + s + 1)
                dve.scalar_tensor_tensor(probs[:, s % 2, :], bank_of(("S", s))[:, 0:384], 0.0, probs[:, s % 2, :],
                                         ALU.max, ALU.add).then_inc(probs_ready, 1)

            def o_lo(l, p):
                dve.wait_ge(o_hi_ready, l * 8 + p + 1)
                dve.tensor_tensor(oT_lo[:, p, :], bank_of(("O", p))[:, 0:256], oT_hi[:, p, :].bitcast(F32),
                                  ALU.subtract).then_inc(drained_of(("O", p)), 1)

            def merge(l, n, q):
                job = ("proj", n, q)
                g = gates[:, 4 * PROJ_ORDER[n] + q, :]
                m = qk_region[:, 512 * q:512 * q + 512]
                wait_filled(dve, l, job)
                if n == 0:
                    dve.tensor_tensor(m, bank_of(job)[:, :], g, ALU.mult).then_inc(drained_of(job), 1)
                    return
                k = 4 * (n - 1) + q
                if k >= 3:
                    dve.wait_ge(*((pool_sums, l * 8 + k - 2) if k <= 10 else (merged_ready, l * 4 + 1)))
                dve.tensor_tensor(product[:, k % 3, :], bank_of(job)[:, :], g, ALU.mult).then_inc(drained_of(job), 1)
                if n == N_BRANCH - 1:
                    wait_drained(dve, l, job)
                    dve.wait_ge(pool_sums, l * 8 + 4 + q + 1)
                    dve.tensor_tensor(m, m, product[:, k % 3, :], ALU.add).then_inc(merged_ready, 1)

            def merged_lo(l, q):
                dve.wait_ge(a_hi_ready, l * 12 + 4 + q + 1)
                dve.tensor_tensor(aT_lo[:, 2 * q:2 * q + 2, :], merged[:, 2 * q:2 * q + 2, :],
                                  aT_hi[:, 2 * q:2 * q + 2, :].bitcast(F32), ALU.subtract)\
                   .then_inc(merged_lo_ready, 1)

            with dve.Fori(0, DEPTH) as l:
                dve.sem_clear(dve_link)
                first_norm(l)
                dve.wait_ge(gains_loaded, l * 32 + 32)
                for c in range(C_GATE):
                    if c == 4:
                        evac_group(l, 0)
                        for tt in range(TT):
                            wait_drained(dve, l, ("group", 0, tt))
                        dve.tensor_scalar(idx_w[:, :, :], zq[:, :, IW:IW + 8], float(IDX_HEADS) ** -0.5, None, ALU.mult)
                    if c == 6:
                        for tt in range(TT):
                            c_norm_of(l, 2 + tt, tt, CKV, MLA_Q, MLA_KV, GAIN_KV)
                        evac_group(l, 1)
                        evac_t(l, "ik", ikT, w=256)
                    if c == 7:
                        for tt in range(TT):
                            c_norm_of(l, 4 + tt, tt, CQ, 0, MLA_Q, GAIN_Q)
                    if c == 8:
                        evac_group(l, 2)
                        c_lo(l, "ckv", 2, 1)
                    if c == 9:
                        evac_t(l, "sk", skT)
                        c_lo(l, "cq", 0, 2)
                    if c == 10:
                        evac_group(l, 3)
                    if c == 12:
                        evac_group(l, 4)
                    if c == 13:
                        evac_uq(dve, l, 1)
                    if c == 14:
                        evac_ukv(dve, l, 1)
                        index_scores(l, 1)
                    if c == 15:
                        index_scores(l, 0)
                    if c >= 1:
                        split_lo(l, c + 2)
                evac_group(l, 5)
                evac_t(l, "mk", mkT)
                for h in range(2):
                    evac_t(l, f"mlak{h}", mla_kT[0:MLA_QK, 2 * h:2 * h + 2, :], rows=MLA_QK)
                for s in range(16):
                    if s >= 4:
                        head_max(l, s)
                    if 1 <= s <= 8:
                        top_round(s - 1)
                    if s == 9:
                        index_mask()
                    if s < 4:
                        softplus(l, s)
                    else:
                        head_norm(l, s)
                    if s == 1:
                        evac_t(l, "dk", dkT)
                    if s >= 3 and s % 2 == 1:
                        o_lo(l, (s - 2) // 2)
                    split_lo(l, C_GATE + s + 2)
                for n in range(N_BRANCH):
                    if n == 1:
                        o_lo(l, 7)
                    dve.wait_ge(gates_ready, l * 4 + n + 1)
                    for q in range(4):
                        merge(l, n, q)
                        if n == N_BRANCH - 1 and q >= 1:
                            merged_lo(l, q - 1)
                        if (n, q) in ((0, 3), (1, 2), (2, 1)):
                            split_lo(l, C_BRANCH + n + 2)
                merged_lo(l, 3)
                dve.wait_ge(lo_ready, l * NCH + RING + C_OUT + 2)
                for k in range(3):
                    split_lo(l, C_OUT + k + 2)
                second_norm(l)

                def u_lo(k):
                    job = ("up", k)
                    dve.wait_ge(u_hi_ready, l * FF_STEPS + k + 1)
                    dve.tensor_tensor(uT_lo[:, k, :], bank_of(job)[:, :], uT_hi[:, k, :].bitcast(F32),
                                      ALU.subtract).then_inc(drained_of(job), 1)

                tok_square(l, 1, 0)
                u_lo(0)
                tok_square(l, 1, 1)
                split_lo(l, C_MLP + 3)
                u_lo(1)
                for c in (4, 5, 6):
                    split_lo(l, C_MLP + c)

                def mlp(k, i=None):
                    more = 0 if i is None else i
                    job = ("up", k)
                    dve.wait_ge(relu_ready, l * (FF_STEPS - 2) + k - 1 + 3 * more)
                    dve.scalar_tensor_tensor(act_sq[:, k % 3, :], bank_of(job)[:, :], 0.0, act_sq[:, k % 3, :],
                                             ALU.max, ALU.mult).then_inc(drained_of(job), 1)
                    if C_MLP + 3 + 2 * k < NCH:
                        split_lo(l, C_MLP + 3 + 2 * k, i)
                    dve.wait_ge(u_hi_ready, l * FF_STEPS + k + 1 + 3 * more)
                    dve.tensor_tensor(uT_lo[:, k % 3, :], act_sq[:, k % 3, :], uT_hi[:, k % 3, :].bitcast(F32),
                                      ALU.subtract).then_inc(u_lo_ready, 1)
                    if C_MLP + 4 + 2 * k < NCH:
                        split_lo(l, C_MLP + 4 + 2 * k, i)

                with dve.Fori(0, 4) as i:
                    for k in (2, 3, 4):
                        mlp(k, i)
                for k in (14, 15):
                    mlp(k)
            last_norm()

        @block.tensor
        def _(pe):
            pe.wait_ge(consts_loaded, 16)

            def products(dst, a_hi, a_lo, b_hi, b_lo, start, stop):
                pe.matmul(dst, a_hi, b_lo, start=start, stop=False)
                pe.matmul(dst, a_hi, b_hi, start=False, stop=False)
                return pe.matmul(dst, a_lo, b_hi, start=False, stop=stop)

            def wait_chunk(l, c, i=None):
                pe.wait_ge(lo_ready, l * NCH + RING + c + 1 + (0 if i is None else i * 6))

            def weights(c, width):
                n = chunk_width(c)
                return [w[:, c % RING, 0:n].rearrange("p (k f) -> p k f", f=width) for w in (w_hi, w_lo)]

            def x_transposes(l, name, n, tt, later=0):
                for q in (2 * tt, 2 * tt + 1):
                    job = (name, q)
                    pe.wait_ge(normed_ready, l * NORMED + NORMED * later + n + q + 1)
                    wait_empty(pe, l, job, FILLS[JOBS[job][0]] * later)
                    for k in range(4):
                        at = P * (4 * (q % 2) + k)
                        last = pe.transpose(bank_of(job)[:, P * k:P * k + P], xn[:, tt, at:at + P], ident)
                    last.then_inc(filled_of(job), 1)

            def group_part(l, c, tt):
                _, g, part = CHUNKS[c]
                width, per_part = GROUP_W[g], KT // parts_of(g)
                hi, lo = weights(c, width)
                if tt == 0:
                    wait_chunk(l, c)
                job = ("group", g, tt)
                if part == 0:
                    wait_empty(pe, l, job)
                if g == 0:
                    wait_drained(pe, l, ("hT", 2 * tt + part // 2))
                for kk in range(per_part):
                    k, t = per_part * part + kk, slice(P * tt, P * tt + P)
                    last = products(bank_of(job)[:, 0:width], aT_hi[:, k, t], aT_lo[:, k, t],
                                    hi[:, kk, :], lo[:, kk, :], k == 0, k == KT - 1)
                if part == parts_of(g) - 1:
                    last.then_inc(filled_of(job), 1)
                elif tt == 1:
                    last.then_inc(chunk_used, 1)

            def latent(l, c, name, width, first, n):
                hi, lo = weights(c, width)
                wait_chunk(l, c)
                for tt in range(TT):
                    job = (name, tt)
                    wait_read(pe, l, [("T", "cq" if name == "uq" else "ckv")], empty=job)
                    t = slice(P * tt, P * tt + P)
                    for k in range(n):
                        last = products(bank_of(job)[:, 0:width], cT_hi[:, first + k, t], cT_lo[:, first + k, t],
                                        hi[:, k, :], lo[:, k, :], k == 0, k == n - 1)
                    last.then_inc(filled_of(job), 1)

            def transposes(l, name, blocks):
                job = ("T", name)
                wait_empty(pe, l, job)
                for n, block_of in enumerate(blocks):
                    for tt in range(TT):
                        src = block_of(tt)
                        last = pe.transpose(bank_of(job)[0:src.shape[1], 256 * n + P * tt:256 * n + P * tt + P], src, ident)
                last.then_inc(filled_of(job), 1)

            def z_blocks(at, n=2):
                return [lambda tt, a=at + P * k: zq[:, tt, a:a + P] for k in range(n)]

            def wait_group(l, g):
                for tt in range(TT):
                    wait_drained(pe, l, ("group", g, tt))

            def index_products(l, qt):
                w = P * (qt + 1)
                for r in range(4):
                    job = ("idx", qt, r)
                    wait_read(pe, l, [("T", "iq"), ("T", "ik")] if (qt, r) == (1, 0) else [], empty=job)
                    rows = slice(32 * r, 32 * r + 32)
                    for b in range(2):
                        last = pe.matmul(bank_of(job)[:, w * b:w * b + w], iqT[rows, b, P * qt:P * qt + P],
                                         ikT[rows, 0:w], start=True, stop=True)
                    last.then_inc(filled_of(job), 1)

            def head_operands(s):
                kind, h = s // 4, s % 4
                if kind == MLA_KIND:
                    return mla_qT[0:MLA_QK, h, :], mla_kT[0:MLA_QK, h, :]
                q, k = {SB_KIND: (sqT, skT), MOBA_KIND: (mqT, mkT), DSA_KIND: (dqT, dkT)}[kind]
                rows = slice(64 * (h % 2), 64 * (h % 2) + 64)
                return q[rows, h // 2, :], k[rows, h // 2, :]

            def head_logits(l, s):
                job = ("S", s)
                S, (q, k) = bank_of(job), head_operands(s)
                kind = s // 4
                names = ()
                if s % 4 == 0:
                    names = {SB_KIND: ("sq", "sk"), MOBA_KIND: ("mq", "mk"),
                             MLA_KIND: ("mlaq0", "mlaq1", "mlak0", "mlak1"), DSA_KIND: ("dq", "dk")}[kind]
                    if kind == DSA_KIND:
                        pe.wait_ge(mask_ready, l + 1)
                if s == 0:
                    pe.wait_ge(const_ready, 1)
                wait_read(pe, l, [("T", name) for name in names], empty=job)
                if kind == SB_KIND:
                    pe.matmul(S[:, 0:256], k[:, 0:128], q[:, 0:256], start=True, stop=False, skip_group_check=True)
                    pe.matmul(S[:, 256:384], k[:, 128:256], q[:, 128:256], start=False, stop=False, skip_group_check=True)
                    pe.matmul(S[:, 0:128], ident_bf[:, :], past_bf[:, :], start=False, stop=False, skip_group_check=True)
                    last = pe.matmul(S[:, 256:384], ident_bf[:, :], past_bf[:, :], start=False, stop=False,
                                     skip_group_check=True)
                else:
                    pe.matmul(S[:, 0:128], q[:, 0:128], k[:, 0:128], start=True, stop=False)
                    pe.matmul(S[:, 0:128], ident_bf[:, :],
                              dsa_mask[:, 0:128] if kind == DSA_KIND else causal_bf[:, :], start=False, stop=True)
                    pe.matmul(S[:, 128:384], q[:, 128:256], k[:, 0:256], start=True, stop=False)
                    if kind == DSA_KIND:
                        last = pe.matmul(S[:, 128:384], ident_bf[:, :], dsa_mask[:, 128:384], start=False, stop=True)
                    else:
                        last = pe.matmul(S[:, 256:384], ident_bf[:, :], causal_bf[:, :], start=False, stop=True)
                last.then_inc(filled_of(job), 1)

            def head_turn(l, s):
                pe.wait_ge(probs_ready, l * 16 + s + 1)
                pr = probs[:, s % 2, :]
                if s // 4 == SB_KIND:
                    S = bank_of(("S", s))
                    pe.matmul(S[:, 0:256], negsuf, pr[:, 0:256], start=False, stop=False, skip_group_check=True)
                    pe.matmul(S[:, 128:256], negones, pr[:, 256:384], start=False, stop=False, skip_group_check=True)
                    pe.matmul(S[:, 256:384], negsuf, pr[:, 256:384], start=False, stop=True, skip_group_check=True)\
                      .then_inc(cum_done, 1)
                    return
                job = ("PT", s)
                wait_empty(pe, l, job)
                for n in range(3):
                    last = pe.transpose(bank_of(job)[:, P * n:P * n + P], pr[:, P * n:P * n + P], ident)
                last.then_inc(filled_of(job), 1)

            def head_values(l, s):
                kind, h = s // 4, s % 4
                job = ("O", s // 2)
                wait_read(pe, l, [("S", s) if kind == SB_KIND else ("PT", s)], empty=job if s % 2 == 0 else None)
                v = v_mla if kind == MLA_KIND else values[:, :, {SB_KIND: 0, MOBA_KIND: 1, DSA_KIND: 2}[kind], :]
                cols = slice(64 * h, 64 * h + 64)
                o = bank_of(job)[64 * (s % 2):64 * (s % 2) + 64, :]
                pT = probsT[:, s % 2, :]
                pe.matmul(o[:, 0:256], v[:, 0, cols], pT[:, 0:256], start=True, stop=False)
                pe.matmul(o[:, 128:256], v[:, 1, cols], pT[:, 256:384], start=False, stop=True)\
                  .then_inc(filled_of(job) if s % 2 else first_of_pair, 1)

            def one_tile(c, dst, a_hi, a_lo, k_tiles, tile):
                cols = slice(P * tile, P * tile + P)
                hi, lo = weights(c, chunk_width(c) // k_tiles)
                for k in range(k_tiles):
                    pe.matmul(dst, hi[:, k, cols], a_lo[:, k, :], start=k == 0, stop=False)
                    pe.matmul(dst, hi[:, k, cols], a_hi[:, k, :], start=False, stop=False)
                    last = pe.matmul(dst, lo[:, k, cols], a_hi[:, k, :], start=False, stop=k == k_tiles - 1)
                return last

            def two_tiles(c, job, a_hi, a_lo, k_tiles, first):
                for f in range(2):
                    last = one_tile(c, bank_of(job)[:, 256 * f:256 * f + 256], a_hi, a_lo, k_tiles, first + f)
                last.then_inc(filled_of(job), 1)

            x_transposes(0, "hT", 0, 0)
            with pe.Fori(0, DEPTH) as l:
                for c in range(2):
                    group_part(l, c, 0)
                x_transposes(l, "hT", 0, 1)
                group_part(l, 2, 0)
                for c in range(3):
                    group_part(l, c, 1)
                for c in range(QUARTERS - 1, C_GATE):
                    if CHUNKS[c][0] == "group":
                        for tt in range(TT):
                            group_part(l, c, tt)
                    elif CHUNKS[c][0] == "uq":
                        latent(l, c, "uq", HEADS * MLA_QK, 0, 2)
                    else:
                        latent(l, c, "ukv", HEADS * 2 * MLA_NOPE, 2, 1)
                    if c == 5:
                        wait_group(l, 0)
                        transposes(l, "sq", z_blocks(SQ))
                        pe.wait_ge(roped, l * ROPES + ONE + 1)
                        transposes(l, "ik", [lambda tt: ik_rep[:, tt, :, :].rearrange("p r d -> p (r d)")])
                    if c == 7:
                        pe.wait_ge(normed_ready, l * NORMED + 6)
                        transposes(l, "ckv", [lambda tt: c_norm[:, tt, MLA_Q:MLA_Q + MLA_KV]])
                    if c == 8:
                        wait_group(l, 2)
                        transposes(l, "sk", z_blocks(SK))
                        pe.wait_ge(normed_ready, l * NORMED + 8)
                        transposes(l, "cq", [lambda tt, a=P * k: c_norm[:, tt, a:a + P] for k in range(2)])
                    if c == 12:
                        pe.wait_ge(roped, l * ROPES + ONE + 3)
                        transposes(l, "iq", z_blocks(IQ))
                    if c in (13, 14):
                        index_products(l, 14 - c)
                pe.wait_ge(roped, l * ROPES + ONE + 4)
                transposes(l, "mq", z_blocks(MQ))
                transposes(l, "mk", z_blocks(MK))
                pe.wait_ge(roped, l * ROPES + ONE + 5)
                for tt in range(TT):
                    wait_drained(pe, l, ("ukv", tt))

                def cat_transposes(name, cat):
                    for h in range(2):
                        transposes(l, f"{name}{h}", [lambda tt, a=MLA_QK * (2 * h + k), c=cat: c[:, tt, a:a + MLA_QK]
                                                     for k in range(2)])

                cat_transposes("mlaq", q_cat)
                for s in range(16):
                    head_logits(l, s)
                    if s == 0:
                        cat_transposes("mlak", k_cat)
                    wait_chunk(l, C_GATE + s)
                    wait_empty(pe, l, ("gate", s))
                    two_tiles(C_GATE + s, ("gate", s), aT_hi, aT_lo, KT, 0)
                    if s == 0:
                        pe.wait_ge(roped, l * ROPES + ONE + 6)
                        transposes(l, "dq", z_blocks(DQ))
                        transposes(l, "dk", z_blocks(DK))
                    head_turn(l, s)
                    if s >= 1:
                        head_values(l, s - 1)
                for n in range(N_BRANCH):
                    wait_chunk(l, C_BRANCH + n)
                    wait_drained(pe, l, ("O", 2 * n + 1))
                    for q in range(4):
                        job = ("proj", n, q)
                        wait_empty(pe, l, job)
                        two_tiles(C_BRANCH + n, job, oT_hi[:, 2 * n:2 * n + 2, :], oT_lo[:, 2 * n:2 * n + 2, :], 2, 2 * q)
                    if n == 0:
                        head_values(l, 15)
                def out_product(c, tt, kk):
                    _, half, kh = CHUNKS[c]
                    hi, lo = weights(c, 512)
                    job, k, t = ("out", half, tt), 4 * kh + kk, slice(P * tt, P * tt + P)
                    last = products(bank_of(job)[:, :], aT_hi[:, k, t], aT_lo[:, k, t],
                                    hi[:, kk, :], lo[:, kk, :], k == 0, k == KT - 1)
                    if k == KT - 1:
                        last.then_inc(filled_of(job), 1)
                    return last

                for tt in range(TT):
                    wait_empty(pe, l, ("out", 0, tt))
                for c in (C_OUT, C_OUT + 1):
                    wait_chunk(l, c)
                    for kk in range(4):
                        if kk % 2 == 0:
                            pe.wait_ge(merged_lo_ready, l * 4 + 2 * (c - C_OUT) + kk // 2 + 1)
                        for tt in range(TT):
                            last = out_product(c, tt, kk)
                    if c == C_OUT:
                        last.then_inc(chunk_used, 1)
                for tt in range(TT):
                    wait_empty(pe, l, ("out", 1, tt))
                    for c in (C_OUT + 2, C_OUT + 3):
                        if tt == 0:
                            wait_chunk(l, c)
                        for kk in range(4):
                            if (tt, c, kk) == (1, C_OUT + 3, 2):
                                x_transposes(l, "h2T", 8, 0)
                            last = out_product(c, tt, kk)
                        if tt == 1 and c == C_OUT + 2:
                            last.then_inc(chunk_used, 1)
                def up(j, i=None):
                    more = 0 if i is None else i
                    c = C_MLP - 1 + 2 * j
                    wait_chunk(l, c, i)
                    wait_empty(pe, l, ("up", j), more)
                    two_tiles(c, ("up", j), aT_hi, aT_lo, KT, 0)

                def down_part(j, tt, half):
                    c = C_MLP + 2 + 2 * j if j < FF_STEPS - 1 else NCH - 1
                    hi, lo = weights(c, D_MODEL)
                    job = ("down", tt, half)
                    for k in range(2):
                        t = slice(256 * k + P * tt, 256 * k + P * tt + P)
                        cols = slice(512 * half, 512 * half + 512)
                        last = products(bank_of(job)[:, :], uT_hi[:, j % 3, t], uT_lo[:, j % 3, t],
                                        hi[:, k, cols], lo[:, k, cols], j == 0 and k == 0, j == FF_STEPS - 1 and k == 1)
                    if j == FF_STEPS - 1:
                        last.then_inc(filled_of(job), 1)
                    elif (tt, half) == (1, 1):
                        last.then_inc(chunk_used, 1)

                def wait_down(j, i=None):
                    wait_chunk(l, C_MLP + 2 + 2 * j if j < FF_STEPS - 1 else NCH - 1, i)
                    if j < 2:
                        wait_drained(pe, l, ("up", j))
                    else:
                        pe.wait_ge(u_lo_ready, l * (FF_STEPS - 2) + j - 1 + (0 if i is None else 3 * i))

                def down(j, i=None):
                    wait_down(j, i)
                    for tt in range(TT):
                        for half in range(2):
                            down_part(j, tt, half)

                def tok_up(tt, j, within=None):
                    job, (hi, lo) = ("utok", tt, j), weights(C_MLP + j, 256)
                    t = slice(P * tt, P * tt + P)
                    wait_chunk(l, C_MLP + j)
                    wait_empty(pe, l, job)
                    for k in range(KT):
                        if j == 0 and k % 4 == 0:
                            wait_drained(pe, l, ("h2T", 2 * tt + k // 4))
                        if k == 4 and within is not None:
                            within()
                        last = products(bank_of(job)[:, 0:256], aT_hi[:, k, t], aT_lo[:, k, t],
                                        hi[:, k, :], lo[:, k, :], k == 0, k == KT - 1)
                    last.then_inc(filled_of(job), 1)

                def u_transposes(j, tts):
                    job = ("up", j)
                    if 0 in tts:
                        wait_empty(pe, l, job)
                    for tt in tts:
                        wait_drained(pe, l, ("utok", tt, j))
                        for f in range(2):
                            at = 256 * j + P * f
                            last = pe.transpose(bank_of(job)[:, 256 * f + P * tt:256 * f + P * tt + P],
                                                act_sq[:, tt, at:at + P], ident)
                    if 1 in tts:
                        last.then_inc(filled_of(job), 1)

                tok_up(0, 0)
                tok_up(0, 1, within=lambda: x_transposes(l, "h2T", 8, 1))
                tok_up(1, 0)
                u_transposes(0, (0,))
                tok_up(1, 1, within=lambda: u_transposes(0, (1,)))
                wait_down(0)
                for tt in range(TT):
                    for half in range(2):
                        down_part(0, tt, half)
                    if tt == 0:
                        u_transposes(1, (0, 1))
                up(2)
                down(1)
                with pe.Fori(0, 4) as i:
                    for j in (2, 3, 4):
                        up(j + 1, i)
                        down(j, i)
                up(15)
                for tt in range(TT):
                    for j in (14, 15):
                        if tt == 0:
                            wait_down(j)
                        for half in range(2):
                            if (tt, j, half) == (1, 15, 1):
                                x_transposes(l, "hT", 0, 0, later=1)
                            down_part(j, tt, half)


_SHAPES = ["x", "w_small", "w_big", "gains", "gate_bias", "consts"]


def kernel(**inputs):
    import numpy as np
    import concourse.bacc as bacc
    from concourse.bass_utils import run_bass_kernel_spmd

    w = {k: np.asarray(v) for k, v in inputs.items()}
    f32 = np.float32

    def tiles(a):
        return a.reshape(-1, P, a.shape[1]).transpose(1, 0, 2).reshape(P, -1)

    w_small = np.empty((DEPTH, SMALL_AT[-1]), f32)
    w_big = np.empty((DEPTH, NCH - C_GATE, P, CW), f32)
    for l in range(DEPTH):
        for c, (kind, *n) in enumerate(CHUNKS):
            if kind == "group":
                rows = D_MODEL // parts_of(n[0])
                a = np.concatenate([w["w_in"][l, rows * n[1]:rows * n[1] + rows, first:first + width]
                                    for first, width in GROUPS[n[0]]], axis=1)
            elif kind == "uq":
                a = w["w_uq"][l]
            elif kind == "ukv":
                a = w["w_ukv"][l]
            elif kind == "gate":
                a = w["w_in"][l, :, GATE0 + 256 * n[0]:GATE0 + 256 * n[0] + 256]
            elif kind == "branch":
                a = w["w_branch"][l, PROJ_ORDER[n[0]]]
            elif kind == "out":
                a = w["w_out"][l, 512 * n[1]:512 * n[1] + 512, 512 * n[0]:512 * n[0] + 512]
            elif kind == "up":
                a = w["w_up"][l, :, 256 * n[0]:256 * n[0] + 256]
            else:
                a = w["w_down"][l, 256 * n[0]:256 * n[0] + 256, :]
            if c < C_GATE:
                w_small[l, SMALL_AT[c]:SMALL_AT[c + 1]] = tiles(a).ravel()
            else:
                w_big[l, c - C_GATE] = tiles(a)

    gains = np.empty((DEPTH + 1, GAIN_W), f32)
    bias = np.empty((DEPTH + 1, P, 32), f32)
    for l in range(DEPTH + 1):
        n = min(l, DEPTH - 1)
        gains[l, GAIN_MIX:GAIN_MLP] = w["norm_mix"][n] if l < DEPTH else w["norm_final"]
        gains[l, GAIN_MLP:GAIN_Q] = w["norm_mlp"][n]
        gains[l, GAIN_Q:GAIN_KV] = w["mla_q_norm"][n]
        gains[l, GAIN_KV:GAIN_W] = w["mla_kv_norm"][n]
        bias[l] = w["b_gate"][n].reshape(32, P).T

    consts = np.zeros((P, CONST_W), f32)
    r = np.arange(P)

    def put(name, a):
        consts[:, CONST_AT[name]:CONST_AT[name] + CONSTS[name]] = a

    put("ident", r[:, None] == r[None, :])
    put("negsuf", -(r[:, None] >= r[None, :]).astype(f32))
    put("negones", -1.0)
    put("causal", np.where(r[None, :] > r[:, None], NEG, 0.0))
    put("past", np.where(r[:, None] >= r[None, :], NEG, 0.0))
    tables = []
    for n_rot in (HEAD_DIM // 4, IDX_DIM // 4, MLA_ROPE):
        inv = (1.0 / (ROPE_THETA ** (np.arange(0, n_rot, 2, dtype=f32) / f32(n_rot)))).astype(f32)
        ang = (np.arange(SEQ, dtype=f32)[:, None] * inv[None, :]).astype(f32)
        tables += [np.cos(ang), np.sin(ang)]
    table = np.concatenate(tables, axis=1).astype(f32)
    put("rope", table.reshape(TT, P, 56).transpose(1, 0, 2).reshape(P, TT * 56))
    put("num", np.array([NORM_EPS, -0.5, 1.0], f32)[None, :])

    nc = bacc.Bacc("TRN2", target_bir_lowering=False, num_devices=1)
    arrays, args = {}, []
    for name, a in zip(_SHAPES, (w["x"], w_small, w_big, gains, bias, consts)):
        arrays[name] = np.ascontiguousarray(a)
        args.append(nc.dram_tensor(name, a.shape, mybir.dt.from_np(a.dtype), kind="ExternalInput").ap())
    args.append(nc.dram_tensor("out", (1, SEQ, D_MODEL), mybir.dt.float32, kind="ExternalOutput").ap())
    build(nc, *args)
    result = run_bass_kernel_spmd(nc, [arrays], core_ids=[0])
    return result.results[0]["out"]
```
